# Optimizing a Trainium2 kernel written in Bass

```python
import jax, jax.numpy as jnp
from jax import lax
import numpy as np

D_MODEL = 1024
BATCH = 1
SEQ = 128
DEPTH = 1
DEC_BATCH = 1
DEC_SEQ = 512
PAST_LEN = 128

GRID_W = 64
HEAD_DIM = 64
N_Q_HEADS = 8
N_KV_HEADS = 2
GROUP = N_Q_HEADS // N_KV_HEADS
ATTN_WIDTH = N_Q_HEADS * HEAD_DIM
KV_WIDTH = N_KV_HEADS * HEAD_DIM
RG_WIDTH = D_MODEL - ATTN_WIDTH
RG_BLOCKS = 8
RG_BLOCK = RG_WIDTH // RG_BLOCKS
CONV_W = 4
C_LRU = 8.0
N_EXPERTS = 16
CAP_FACTOR = 2
D_EXPERT = 1024
Q_BLOCK = 128
ROPE_THETA = 10000.0
NORM_EPS = 1e-6
ALPHA = (2.0 * DEPTH) ** 0.25
BETA = (8.0 * DEPTH) ** -0.25
IN_WIDTH = ATTN_WIDTH + 2 * KV_WIDTH + 2 * RG_WIDTH

kernel_name = "hybrid_gqa_rglru_ec_moe_diffusion_step"

def layer_norm_plain(x):
    xf = x.astype(jnp.float32)
    mu = jnp.mean(xf, -1, keepdims=True)
    var = jnp.mean(jnp.square(xf - mu), -1, keepdims=True)
    return (xf - mu) * lax.rsqrt(var + NORM_EPS)

def layer_norm(x, g, b):
    y = layer_norm_plain(x) * g.astype(jnp.float32) + b.astype(jnp.float32)
    return y.astype(x.dtype)

def rms_norm(x, g):
    xf = x.astype(jnp.float32)
    y = xf * lax.rsqrt(jnp.mean(jnp.square(xf), -1, keepdims=True) + NORM_EPS)
    return (y * g.astype(jnp.float32)).astype(x.dtype)

def modulate(x, shift, scale):
    return (layer_norm_plain(x) * (1.0 + scale.astype(jnp.float32)) + shift.astype(jnp.float32)).astype(x.dtype)

def rope_half(x, pos):
    nf = x.shape[-1] // 2
    inv = ROPE_THETA ** (-jnp.arange(nf, dtype=jnp.float32) / nf)
    ang = pos.astype(jnp.float32)[:, None] * inv[None, :]
    cos = jnp.cos(ang)[None, :, None, :]
    sin = jnp.sin(ang)[None, :, None, :]
    x1, x2 = x[..., :nf], x[..., nf:]
    return jnp.concatenate([x1 * cos - x2 * sin, x1 * sin + x2 * cos], -1)

def axial_rope(x):
    n = x.shape[1]
    rows = n // GRID_W
    row = jnp.broadcast_to(jnp.arange(rows)[:, None], (rows, GRID_W)).reshape(n)
    col = jnp.broadcast_to(jnp.arange(GRID_W)[None, :], (rows, GRID_W)).reshape(n)
    xf = x.astype(jnp.float32)
    half = HEAD_DIM // 2
    y = jnp.concatenate([rope_half(xf[..., :half], row), rope_half(xf[..., half:], col)], -1)
    return y.astype(x.dtype)

def block_attention(q, k, v):
    b, n = q.shape[:2]
    nblk = n // Q_BLOCK
    qb = jnp.moveaxis(q.reshape(b, nblk, Q_BLOCK, N_KV_HEADS, GROUP, HEAD_DIM), 1, 0)
    scale = HEAD_DIM ** -0.5

    def one_block(qblk):
        s = jnp.einsum('bqhgd,bkhd->bhgqk', qblk, k, preferred_element_type=jnp.float32) * scale
        p = jax.nn.softmax(s, axis=-1).astype(v.dtype)
        return jnp.einsum('bhgqk,bkhd->bqhgd', p, v)

    o = lax.map(one_block, qb)
    return jnp.moveaxis(o, 0, 1).reshape(b, n, ATTN_WIDTH)

def centred_conv(x, w, b):
    n = x.shape[1]
    left = CONV_W // 2
    xp = jnp.pad(x, ((0, 0), (left, CONV_W - 1 - left), (0, 0)))
    return sum(xp[:, j:j + n] * w[j] for j in range(CONV_W)) + b

def block_diag(x, w, b):
    xb = x.reshape(x.shape[:-1] + (RG_BLOCKS, RG_BLOCK))
    return jnp.einsum('bnhi,hij->bnhj', xb, w).reshape(x.shape) + b

def rglru_coeffs(x, w_a, b_a, w_x, b_x, lam):
    r = jax.nn.sigmoid(block_diag(x, w_a, b_a).astype(jnp.float32))
    i = jax.nn.sigmoid(block_diag(x, w_x, b_x).astype(jnp.float32))
    log_a = -C_LRU * r * jax.nn.softplus(-lam.astype(jnp.float32))
    a = jnp.exp(log_a)
    bx = jnp.sqrt(-jnp.expm1(2.0 * log_a)) * (i * x.astype(jnp.float32))
    return a, bx

def linear_scan(a, bx, h0, reverse):
    def combine(l, r):
        return l[0] * r[0], r[0] * l[1] + r[1]
    acum, bcum = lax.associative_scan(combine, (a, bx), axis=1, reverse=reverse)
    return acum * h0.astype(jnp.float32)[:, None, :] + bcum

def token_mixer(h, w_in, q_g, k_g, conv_w, conv_b, w_a, b_a, w_x, b_x, lam, w_out, ctx):
    B, N, _ = h.shape
    z = h @ w_in
    q, k, v, xr, gr = jnp.split(z, [ATTN_WIDTH, ATTN_WIDTH + KV_WIDTH, ATTN_WIDTH + 2 * KV_WIDTH,
                                     ATTN_WIDTH + 2 * KV_WIDTH + RG_WIDTH], axis=-1)
    q = rms_norm(q.reshape(B, N, N_Q_HEADS, HEAD_DIM), q_g)
    k = rms_norm(k.reshape(B, N, N_KV_HEADS, HEAD_DIM), k_g)
    v = v.reshape(B, N, N_KV_HEADS, HEAD_DIM)
    xc = centred_conv(xr, conv_w, conv_b)
    if ctx is None:
        keys, vals = k, v
        h0 = jnp.zeros((B, 2, RG_WIDTH), h.dtype)
    else:
        ctx_k, ctx_v, ctx_h = ctx
        q = axial_rope(q)
        keys = jnp.concatenate([axial_rope(k), ctx_k.astype(k.dtype)], axis=1)
        vals = jnp.concatenate([v, ctx_v.astype(v.dtype)], axis=1)
        h0 = ctx_h
    attn = block_attention(q.reshape(B, N, N_KV_HEADS, GROUP, HEAD_DIM), keys, vals)
    a_f, bx_f = rglru_coeffs(xc, w_a[0], b_a[0], w_x[0], b_x[0], lam[0])
    a_b, bx_b = rglru_coeffs(xc, w_a[1], b_a[1], w_x[1], b_x[1], lam[1])
    h_f = linear_scan(a_f, bx_f, h0[:, 0], reverse=False)
    h_b = linear_scan(a_b, bx_b, h0[:, 1], reverse=True)
    rg = (h_f + h_b).astype(h.dtype) * jax.nn.gelu(gr)
    out = jnp.concatenate([attn, rg], axis=-1) @ w_out
    if ctx is None:
        final = jnp.stack([h_f[:, -1], h_b[:, 0]], axis=1).astype(h.dtype)
        return out, (k, v, final)
    return out, None

def expert_choice_ffn(h, w_router, w_gate_up, w_down):
    B, N, D = h.shape
    cap = CAP_FACTOR * N // N_EXPERTS
    aff = jax.nn.softmax((h @ w_router).astype(jnp.float32), axis=-1)
    g, idx = lax.top_k(jnp.swapaxes(aff, 1, 2), cap)
    xs = jax.vmap(lambda hb, ib: hb[ib])(h, idx)
    gu = jnp.einsum('becd,edf->becf', xs, w_gate_up)
    gate, up = jnp.split(gu, 2, axis=-1)
    y = jnp.einsum('becf,efd->becd', jax.nn.silu(gate) * up, w_down) * g[..., None].astype(h.dtype)
    return jax.vmap(lambda ib, yb: jnp.zeros((N, D), yb.dtype).at[ib.reshape(-1)].add(yb.reshape(-1, D)))(idx, y)

def trunk_layer(x, mod, w_in, q_g, k_g, conv_w, conv_b, w_a, b_a, w_x, b_x, lam, w_out,
                ln1_g, ln1_b, w_router, w_gate_up, w_down, ln2_g, ln2_b, ctx):
    shift1, scale1, gate1, shift2, scale2, gate2 = jnp.split(mod, 6, axis=-1)
    mix, new_ctx = token_mixer(modulate(x, shift1, scale1), w_in, q_g, k_g, conv_w, conv_b,
                               w_a, b_a, w_x, b_x, lam, w_out, ctx)
    x = layer_norm(ALPHA * x + gate1 * mix, ln1_g, ln1_b)
    ff = expert_choice_ffn(modulate(x, shift2, scale2), w_router, w_gate_up, w_down)
    x = layer_norm(ALPHA * x + gate2 * ff, ln2_g, ln2_b)
    return x, new_ctx

def setup_inputs(seed: int = 0) -> dict:
    key = jax.random.key(seed)
    ks = jax.random.split(key, 32)
    nrm = lambda k, s, sc: jax.random.normal(k, s, jnp.float32) * sc
    D = D_MODEL
    u = jax.random.uniform(ks[15], (DEPTH, 2, RG_WIDTH), jnp.float32, 0.9, 0.999)
    s = u ** (1.0 / C_LRU)
    rg_lambda = jnp.log(s) - jnp.log1p(-s)
    return {
        'x_prompt': nrm(ks[0], (BATCH, SEQ, D), 1.0),
        'x_sample': nrm(ks[1], (DEC_BATCH, DEC_SEQ, D), 1.0),
        'cache_k': nrm(ks[2], (DEC_BATCH, DEPTH, PAST_LEN, N_KV_HEADS, HEAD_DIM), 1.0),
        'cache_v': nrm(ks[3], (DEC_BATCH, DEPTH, PAST_LEN, N_KV_HEADS, HEAD_DIM), 1.0),
        'state_h': nrm(ks[4], (DEC_BATCH, DEPTH, 2, RG_WIDTH), 0.5),
        'c': nrm(ks[5], (DEC_BATCH, D), 1.0),
        'c_ctx': nrm(ks[6], (D,), 1.0),
        'w_mod': nrm(ks[7], (DEPTH, D, 6 * D), D ** -0.5),
        'b_mod': nrm(ks[8], (DEPTH, 6 * D), 0.02),
        'w_in': nrm(ks[9], (DEPTH, D, IN_WIDTH), D ** -0.5),
        'q_norm_g': 1.0 + nrm(ks[10], (DEPTH, HEAD_DIM), 0.02),
        'k_norm_g': 1.0 + nrm(ks[11], (DEPTH, HEAD_DIM), 0.02),
        'conv_w': nrm(ks[12], (DEPTH, CONV_W, RG_WIDTH), CONV_W ** -0.5),
        'conv_b': nrm(ks[13], (DEPTH, RG_WIDTH), 0.02),
        'w_rg_a': nrm(ks[14], (DEPTH, 2, RG_BLOCKS, RG_BLOCK, RG_BLOCK), RG_BLOCK ** -0.5),
        'b_rg_a': nrm(ks[16], (DEPTH, 2, RG_WIDTH), 0.02),
        'w_rg_x': nrm(ks[17], (DEPTH, 2, RG_BLOCKS, RG_BLOCK, RG_BLOCK), RG_BLOCK ** -0.5),
        'b_rg_x': nrm(ks[18], (DEPTH, 2, RG_WIDTH), 0.02),
        'rg_lambda': rg_lambda,
        'w_out': nrm(ks[19], (DEPTH, D, D), BETA * D ** -0.5),
        'ln1_g': 1.0 + nrm(ks[20], (DEPTH, D), 0.02),
        'ln1_b': nrm(ks[21], (DEPTH, D), 0.02),
        'w_router': nrm(ks[22], (DEPTH, D, N_EXPERTS), D ** -0.5),
        'w_gate_up': nrm(ks[23], (DEPTH, N_EXPERTS, D, 2 * D_EXPERT), D ** -0.5),
        'w_down': nrm(ks[24], (DEPTH, N_EXPERTS, D_EXPERT, D), BETA * D_EXPERT ** -0.5),
        'ln2_g': 1.0 + nrm(ks[25], (DEPTH, D), 0.02),
        'ln2_b': nrm(ks[26], (DEPTH, D), 0.02),
    }

def reference(x_prompt, x_sample, cache_k, cache_v, state_h, c, c_ctx, w_mod, b_mod, w_in,
              q_norm_g, k_norm_g, conv_w, conv_b, w_rg_a, b_rg_a, w_rg_x, b_rg_x, rg_lambda,
              w_out, ln1_g, ln1_b, w_router, w_gate_up, w_down, ln2_g, ln2_b):
    xp = x_prompt
    ks_new, vs_new, hs_new = [], [], []
    for l in range(DEPTH):
        mod = (jax.nn.silu(c_ctx) @ w_mod[l] + b_mod[l])[None, None, :]
        xp, (k_l, v_l, h_l) = trunk_layer(
            xp, mod, w_in[l], q_norm_g[l], k_norm_g[l], conv_w[l], conv_b[l], w_rg_a[l], b_rg_a[l],
            w_rg_x[l], b_rg_x[l], rg_lambda[l], w_out[l], ln1_g[l], ln1_b[l], w_router[l],
            w_gate_up[l], w_down[l], ln2_g[l], ln2_b[l], None)
        ks_new.append(k_l)
        vs_new.append(v_l)
        hs_new.append(h_l)
    new_k = jnp.stack(ks_new, axis=1)
    new_v = jnp.stack(vs_new, axis=1)
    new_h = jnp.stack(hs_new, axis=1)

    xs = x_sample
    for l in range(DEPTH):
        mod = (jax.nn.silu(c) @ w_mod[l] + b_mod[l])[:, None, :]
        xs, _ = trunk_layer(
            xs, mod, w_in[l], q_norm_g[l], k_norm_g[l], conv_w[l], conv_b[l], w_rg_a[l], b_rg_a[l],
            w_rg_x[l], b_rg_x[l], rg_lambda[l], w_out[l], ln1_g[l], ln1_b[l], w_router[l],
            w_gate_up[l], w_down[l], ln2_g[l], ln2_b[l],
            (cache_k[:, l], cache_v[:, l], state_h[:, l]))

    return (xp, xs, new_k, new_v, new_h)


_drawn_inputs = setup_inputs


def setup_inputs(seed=0):
    import zlib

    import numpy as np

    out = dict(_drawn_inputs(seed))
    spreads = {}
    factors = {'cache_k': 7.295,
     'cache_v': 7.531,
     'q_norm_g': 8.0,
     'k_norm_g': 7.863,
     'b_rg_a': 21.993,
     'b_rg_x': 6.879,
     'ln2_b': 2.803}
    for name, (base, spread) in spreads.items():
        noise = np.random.default_rng([zlib.crc32(name.encode()), seed]).standard_normal(out[name].shape)
        drawn = base * np.exp(spread * noise) if base else spread * noise
        out[name] = __import__('jax').numpy.asarray(drawn.astype(out[name].dtype))
    for name, factor in factors.items():
        out[name] = (out[name] * factor).astype(out[name].dtype)
    return out
```

```python
from contextlib import ExitStack

import numpy as np

import concourse.bass as bass
from concourse import mybir

F32 = mybir.dt.float32
F32R = mybir.dt.float32r
U32 = mybir.dt.uint32
ALU = mybir.AluOpType
ACT = mybir.ActivationFunctionType
AX = mybir.AxisListType

P = 128
D = 1024
KC = D // P
N_S, N_P = 512, 128
NT = N_S + N_P
CH = NT // P
PC = CH - 1
PAST = 128
HD, NQ, NKV = 64, 8, 2
QW, KVW = NQ * HD, NKV * HD
QKV = QW + 2 * KVW
RG = 512
RJ = RG // P
NE, CAP_S, CAP_P = 16, 64, 16
SL = CAP_S + CAP_P
FE = 1024
EPS = 1e-6
ALPHA = 2.0 ** 0.25
SCALE = HD ** -0.5
C_LRU = 8.0
MG = 33
GRID_W = 64

RING = 8
WR = 4
GU_PIECES = 8
E_PIECES = 3 * KC
PAIR_PIECES = 2 * E_PIECES
UNITS_A = (16 + 8 + 8 + 32 + 8) // 2

R_C, R_CTX, R_BM, R_CW, R_CB, R_BA, R_BX, R_LAM, R_H0, R_END = 0, 8, 16, 64, 80, 84, 92, 100, 108, 116


def build(nc, t):
    with ExitStack() as ctx:
        _build(nc, ctx, t)


def _build(nc, ctx, t):
    def sem(name):
        return ctx.enter_context(nc.semaphore(name))

    base = -(-nc.sbuf_base // 64) * 64
    RAW = nc.sbuf_usable_end - 200960 - 64
    RAW -= RAW % 64
    Bz, Cz = RAW, RAW + 32768
    Dz = Cz + 20736
    Ez = Dz + 65536
    Fz = Ez + 40960
    assert Fz + 40960 <= nc.sbuf_usable_end
    small = [base]

    def at(name, shape, off, dt=F32):
        return nc.alloc_sbuf_tensor_at(name, shape, dt, offset=off)

    def tile(name, shape, dt=F32):
        n = 4
        for s in shape[1:]:
            n *= s
        off = small[0]
        small[0] += -(-n // 32) * 32
        assert small[0] <= RAW, (name, small[0], RAW)
        return at(name, shape, off, dt)

    consts = tile("consts", [P, P + 256 + NT + CH])
    ident = consts[:, 0:P]
    rope = consts[:, P:P + 256].rearrange("p (c w n) -> p c w n", c=4, w=2)
    iota_tok = consts[:, P + 256:P + 256 + NT]
    tok_id = consts[:, P + 256 + NT:P + 256 + NT + CH]
    cols = tile("cols", [P, R_END])
    cT = tile("cT", [P, KC, MG])
    modT = tile("modT", [P, 4, 2, KC])
    stats = tile("stats", [P, CH, 2, 6])
    mv = tile("mv", [P, CH, 2])
    rstd = tile("rstd", [P, CH])
    ptmp = tile("ptmp", [P, 16])
    mhalf = tile("mhalf", [P, 16])
    ssq = tile("ssq", [P, 2, 10])
    rsq = tile("rsq", [P, 2, 10])
    gqk = tile("gqk", [P, 2, HD])
    w_rt = tile("w_rt", [P, KC, NE])
    nsp = tile("nsp", [P, 3, 8])
    lscr = tile("lscr", [P, 4, 8])
    ones16 = tile("ones16", [NE, P])
    hst_out = tile("hst_out", [P, 2, RJ])
    smax = tile("smax", [P, 2])
    nmax = tile("nmax", [P, 2])
    ssum = tile("ssum", [P, 2])
    rsum = tile("rsum", [P, 2])
    rmax = tile("rmax", [P, CH])
    aff = tile("aff", [P, CH, NE])
    idx_slot = tile("idx_slot", [SL, NE + 1])
    g_slot = tile("g_slot", [SL, NE + 1])
    topv = tile("topv", [NE, SL])
    topi = tile("topi", [NE, SL], U32)
    topf = tile("topf", [NE, SL])

    ring = at("ring", [P, RING, 1024], Bz)
    xt = at("xt", [P, CH, D], Cz)
    XRW = 648
    xr = at("xr", [P, RJ, XRW], Cz)
    gel = at("gel", [P, RJ, NT], Cz + 4 * RJ * XRW)
    WAh = at("WAh", [P, KC, 1024], Dz, F32R)
    WAl = at("WAl", [P, KC, 1024], Dz + 32768, F32R)
    B10 = 4 * RJ * NT
    gate_r = [at("gate_r0", [P, RJ, NT], Dz), at("gate_r1", [P, RJ, NT], Ez)]
    gate_i = [at("gate_i0", [P, RJ, NT], Dz + B10), at("gate_i1", [P, RJ, NT], Ez + B10)]
    thx = [at("thx0", [P, RJ, NT], Dz + 2 * B10), at("thx1", [P, RJ, NT], Ez + 2 * B10)]
    hst = [at("hst0", [P, RJ, NT], Dz + 3 * B10), at("hst1", [P, RJ, NT], Dz + 4 * B10)]
    b_row = at("b_row", [MG, D], Dz + 5 * B10)
    m_row = at("m_row", [MG, D], Dz + 5 * B10 + 4096)
    Hh = at("Hh", [P, KC, NT], Ez, F32R)
    Hl = at("Hl", [P, KC, NT], Ez + 20480, F32R)
    qT = at("qT", [P, 4, NT], Fz)
    kT = at("kT", [P, NKV, NT + PAST], Fz + 10240)
    V = at("V", [P, 6, KVW], Fz + 16384)
    Z = Fz + 19456
    m_rowA = [at("m_rowA0", [MG, D], Fz), at("m_rowA1", [MG, D], Fz + 4096)]
    hmod = [at("hmod0", [P, NT], Z), at("hmod1", [P, NT], Z + 2560)]
    sq = at("sq", [P, 640], Z + 5120)
    qn = at("qn", [P, 640], Z + 7680)
    qr = [at("qr0", [P, 640], Z + 10240), at("qr1", [P, 640], Z + 12800)]
    rt = at("rt", [P, 2, 320], Z + 15360)
    kd = [at("kd0", [P, 256], Z + 17920), at("kd1", [P, 256], Z + 18944)]
    ckd = at("ckd", [P, 256], Z + 19968)
    BD = at("BD", [P, 16, P], Z)
    XC = at("XC", [P, RJ, NT], Z + 8192)
    prob = [at("prob0", [P, 640], Z), at("prob1", [P, 640], Z + 2560)]
    PT = at("PT", [P, 5, 512], Z + 5120)
    PTp = at("PTp", [P, P], Z + 15360)
    xn2 = at("xn2", [P, CH, D], Fz)
    h2T = at("h2T", [P, KC, P], Fz + 20480)
    G1 = [at("G1s", [P, D], Fz + 24576), at("G1p", [P, D], Fz + 28672)]
    ln1g = at("ln1g", [P, D], Fz + 32768)
    ln1b = at("ln1b", [P, D], Fz + 36864)
    X2h = at("X2h", [P, CH, D], Dz, F32R)
    X2l = at("X2l", [P, CH, D], Dz + 20480, F32R)
    Ss = at("Ss", [P, 4, NE, CAP_S], Dz + 40960, F32R)
    Sp = at("Sp", [P, NE, CAP_P], Dz + 57344, F32R)
    affw = at("affw", [NE, NT], Ez)
    idxx = at("idxx", [NE, NE, SL], Ez + 2560)
    XS = at("XS", [P, NE, KC, SL], Ez)
    Wh = at("Wh", [P, WR, 1024], Fz, F32R)
    Wl = at("Wl", [P, WR, 1024], Fz + 16384, F32R)
    G2 = at("G2", [SL, D], Fz + 32768)
    ysc = at("ysc", [SL, D], Fz + 36864)
    o = Dz
    Xh, Xl, gate_act, hrow, Yh, Yl, ST = [], [], [], [], [], [], []
    for b in range(2):
        Xh.append(at(f"Xh{b}", [P, KC, SL], o, F32R)); o += 4 * KC * SL
        Xl.append(at(f"Xl{b}", [P, KC, SL], o, F32R)); o += 4 * KC * SL
        gate_act.append(at(f"gate_act{b}", [SL, 512], o)); o += 2048
        hrow.append(at(f"hrow{b}", [SL, 512], o)); o += 2048
        Yh.append(at(f"Yh{b}", [SL, D], o, F32R)); o += 4096
        Yl.append(at(f"Yl{b}", [SL, D], o, F32R)); o += 4096
        ST.append(at(f"ST{b}", [SL, NT], o, F32R)); o += 2560
    HTh = at("HTh", [P, KC, SL], o, F32R); o += 4 * KC * SL
    HTl = at("HTl", [P, KC, SL], o, F32R); o += 4 * KC * SL
    zrow = at("zrow", [P, 512], o); o += 2048
    assert o <= Dz + 65536
    ln2g = at("ln2g", [P, D], Ez)
    ln2b = at("ln2b", [P, D], Ez + 4096)
    osb = at("osb", [P, 2, D], Ez + 8192)

    PS = ctx.enter_context(nc.psum_tensor("PS", [P, 4096], F32))

    def bank(b, lo=0, hi=512, rows=P):
        return PS[0:rows, 512 * b + lo:512 * b + hi]

    rt_w = t["w_router"][0].rearrange("(k p) e -> p k e", p=P)
    w_mod_v = t["w_mod"][0].rearrange("(k p) (g n) -> p k g n", p=P, n=D)
    w_in_v = t["w_in"][0].rearrange("(k p) n -> p k n", p=P)
    w_out_v = t["w_out"][0].rearrange("(k p) n -> p k n", p=P)
    w_gu_v = t["w_gate_up"][0].rearrange("e (k p) (g h n) -> e p k g h n", p=P, g=2, h=2)
    w_dn_v = t["w_down"][0].rearrange("e (k p) n -> e p k n", p=P)
    gates_dram = nc.dram_tensor("gates_scratch", (2, 2, D), F32, kind="Internal").ap()
    y_s = t["y_sample"][0].rearrange("(c p) d -> p c d", p=P)
    x_s = t["x_sample"][0].rearrange("(c p) d -> p c d", p=P)

    rows_in, const_in, misc_in = sem("rows_in"), sem("const_in"), sem("misc_in")
    x_in = [sem(f"x_in{c}") for c in range(CH)]
    x_again = [sem(f"x_again{c}") for c in range(CH)]
    landed = [sem(f"landed{s}") for s in range(RING // 2)]
    cache_in = sem("cache_in")
    rows_t, ct_zero, ct_ok = sem("rows_t"), sem("ct_zero"), sem("ct_ok")
    mod_used, mrow_ok, mrow_t, modT_ok = sem("mod_used"), sem("mrow_ok"), sem("mrow_t"), sem("modT_ok")
    var_ok, rstd_ok, xn_ok = sem("var_ok"), sem("rstd_ok"), sem("xn_ok")
    h_t, hmod_ok, h_lo = sem("h_t"), sem("hmod_ok"), sem("h_lo")
    split_hi, split_lo, wa_used = sem("split_hi"), sem("split_lo"), sem("wa_used")
    q_ps, q_free, sq_ok, v_ok, ss_ok, rs_ok = sem("q_ps"), sem("q_free"), sem("sq_ok"), sem("v_ok"), sem("ss_ok"), sem("rs_ok")
    qr_ok, qk_t, qk_ok = sem("qr_ok"), sem("qk_t"), sem("qk_ok")
    r_ps, r_ok, pads_ok, xc_ok = sem("r_ps"), sem("r_ok"), sem("pads_ok"), sem("xc_ok")
    bd_zero, bd_in, g_ps, g_ok, th_ok, om_ok, sqr_ok = (sem("bd_zero"), sem("bd_in"), sem("g_ps"), sem("g_ok"), sem("th_ok"),
                                                         sem("om_ok"), sem("sqr_ok"))
    rg_ok, h_done = sem("rg_ok"), sem("h_done")
    lam_e, nsp_ok, nb_ok = sem("lam_e"), sem("nsp_ok"), sem("nb_ok")
    brow_zero, brow_in, gate_row, gate_out = sem("brow_zero"), sem("brow_in"), sem("gate_row"), sem("gate_out")
    s_ps, nmax_ok, exp_ok, prob_ok, pt_ps, pt_ok, pv_ps, cat_hi, cat_lo = (
        sem("s_ps"), sem("nmax_ok"), sem("exp_ok"), sem("prob_ok"), sem("pt_ps"), sem("pt_ok"), sem("pv_ps"),
        sem("cat_hi"), sem("cat_lo"))
    out_ps, out_free, g1_in, var2_ok, rstd2_ok, xn2_ok, acc_ok = (
        sem("out_ps"), sem("out_free"), sem("g1_in"), sem("var2_ok"), sem("rstd2_ok"), sem("xn2_ok"), sem("acc_ok"))
    x2_t, h2_ok, lg_ps, lmax_ok, lexp_ok, aff_ok, aff_t = (sem("x2_t"), sem("h2_ok"), sem("lg_ps"), sem("lmax_ok"),
                                                           sem("lexp_ok"), sem("aff_ok"), sem("aff_t"))
    x2_hi, x2_lo, top_t, slot_ok, idxx_ok, idxb_ps, S_ok, ga_ps, ga_ok = (
        sem("x2_hi"), sem("x2_lo"), sem("top_t"), sem("slot_ok"), sem("idxx_ok"), sem("idxb_ps"), sem("S_ok"),
        sem("ga_ps"), sem("ga_ok"))
    g2_in, pre_ok, W_hi, W_lo, W_used = sem("g2_in"), sem("pre_ok"), sem("W_hi"), sem("W_lo"), sem("W_used")
    X_hi, X_lo, act_ok, hrow_ok, ht_ps, ht_hi, ht_lo = (
        sem("X_hi"), sem("X_lo"), sem("act_ok"), sem("hrow_ok"), sem("ht_ps"), sem("ht_hi"), sem("ht_lo"))
    y_ok, y_hi, y_lo, cb_ps, cb_free = sem("y_ok"), sem("y_hi"), sem("y_lo"), sem("cb_ps"), sem("cb_free")
    ln2_in, var3_ok, rstd3_ok, y_out, pool_out = sem("ln2_in"), sem("var3_ok"), sem("rstd3_ok"), sem("y_out"), sem("pool_out")
    stored = [sem("stored0"), sem("stored1")]
    dve_seq, pool_seq, act_seq = sem("dve_seq"), sem("pool_seq"), sem("act_seq")
    hout, ones_ok = sem("hout"), sem("ones_ok")

    def landed_wait(eng, unit):
        eng.wait_ge(landed[unit % 4], 16 * (unit // 4 + 1))

    U_Q, U_R, U_MB, U_O = 8, 12, 16, 32

    block = ctx.enter_context(nc.Block())

    @block.sync
    def _(sp):
        bm_rows = t["b_mod"][0].rearrange("(r p) -> r p", p=P)
        for r0, src in ((R_C, t["c"][0].rearrange("(r p) -> r p", p=P)),
                        (R_CTX, t["c_ctx"].rearrange("(r p) -> r p", p=P)),
                        (R_BM, bm_rows),
                        (R_CW, t["conv_w"][0].rearrange("w (j p) -> (w j) p", p=P)),
                        (R_CB, t["conv_b"][0].rearrange("(j p) -> j p", p=P)),
                        (R_BA, t["b_rg_a"][0].rearrange("d (j p) -> (d j) p", p=P)),
                        (R_BX, t["b_rg_x"][0].rearrange("d (j p) -> (d j) p", p=P)),
                        (R_LAM, t["rg_lambda"][0].rearrange("d (j p) -> (d j) p", p=P)),
                        (R_H0, t["state_h"][0, 0].rearrange("d (j p) -> (d j) p", p=P))):
            sp.dma_start(ring[r0:r0 + src.shape[0], 7, 0:P], src).then_inc(rows_in, 16)
            if r0 == R_C:
                sp.dma_start(consts[:], t["consts"]).then_inc(const_in, 16)

        def stream(u, dst, src):
            v = u - 4
            if u == 3:
                sp.wait_ge(rows_t, 1)
            if v >= U_O:
                sp.wait_ge(split_lo, 16 + 2 * (v - U_O + 1))
            elif v >= U_MB:
                sp.wait_ge(mod_used, 16 + 2 * (v - U_MB + 1))
            elif v >= U_Q:
                sp.wait_ge(split_lo, 2 * (v - U_Q + 1))
            elif v >= 0:
                sp.wait_ge(mod_used, 2 * (v + 1))
            sp.dma_start(dst, src).then_inc(landed[u % 4], 16)

        def slots(u, w=1024):
            return ring[:, 2 * (u % 4):2 * (u % 4) + 2, 0:w]

        for u in range(8):
            stream(u, slots(u), w_mod_v[:, 2 * (u % 4):2 * (u % 4) + 2, u // 4, :])
        for m in range(4):
            stream(U_Q + m, slots(U_Q + m, QKV), w_in_v[:, 2 * m:2 * m + 2, 0:QKV])
            if m == 0:
                sp.dma_start(gqk[:, 0, :], t["q_norm_g"][0].partition_broadcast(P)).then_inc(misc_in, 16)
                sp.dma_start(gqk[:, 1, :], t["k_norm_g"][0].partition_broadcast(P)).then_inc(misc_in, 16)
                sp.dma_start(w_rt[:], rt_w).then_inc(misc_in, 16)
        for m in range(4):
            stream(U_R + m, slots(U_R + m), w_in_v[:, 2 * m:2 * m + 2, QKV:QKV + 2 * RG])
        for m in range(16):
            stream(U_MB + m, slots(U_MB + m), w_mod_v[:, 2 * (m % 4):2 * (m % 4) + 2, 2 + m // 4, :])
        for m in range(4):
            stream(U_O + m, slots(U_O + m), w_out_v[:, 2 * m:2 * m + 2, :])

        def expert_dma(unit, e):
            for m in range(2):
                if unit < 8:
                    src = w_gu_v[e][:, 2 * (unit % 4):2 * (unit % 4) + 2, m, unit // 4, :]
                    dst = ring[:, 2 * (unit % 4):2 * (unit % 4) + 2, 512 * m:512 * m + 512]
                else:
                    src = w_dn_v[e][:, 2 * (unit - 8) + m, :]
                    dst = ring[:, 2 * (unit % 4) + m, :]
                sp.dma_start(dst, src).then_inc(landed[unit % 4], 16)

        for m in range(4):
            sp.wait_ge(split_lo, 16 + 2 * (m + 1))
            expert_dma(m, 0)
        with sp.Fori(0, NE // 2 - 1) as i:
            for m in range(24):
                sp.wait_ge(W_lo, i * PAIR_PIECES + (2 * m + 2))
                expert_dma((m + 4) % 12, 2 * i + (m + 4) // 12)
        for m in range(20):
            sp.wait_ge(W_lo, (NE // 2 - 1) * PAIR_PIECES + 2 * m + 2)
            expert_dma((m + 4) % 12, NE - 2 + (m + 4) // 12)
        for n in range(CH):
            c = n
            sp.wait_ge(y_out, n + 1)
            dst = y_s[:, c, :] if c < PC else t["y_prompt"][0]
            sp.dma_start(dst, osb[:, n % 2, :]).then_inc(stored[n % 2], 16)
        sp.wait_ge(stored[0], 16 * 3)
        sp.wait_ge(stored[1], 16 * 2)

    @block.gpsimd
    def _(pool):
        seq = [0]

        def link(ins):
            seq[0] += 1
            ins.then_inc(pool_seq, 1)
            pool.wait_ge(pool_seq, seq[0])

        def pow_mhalf(out, in_, n, mul):
            link(pool.tensor_scalar(ptmp[:, 0:n], in_, mul, EPS, ALU.mult, ALU.add))
            return pool.tensor_tensor(out, ptmp[:, 0:n], mhalf[:, 0:n], ALU.pow)

        pool.memset(cT[:], 0.0).then_inc(ct_zero, 1)
        link(pool.memset(mhalf[:], -0.5))
        for h in range(2):
            pool.dma_start(ckd[:].rearrange("p (g h d) -> p g h d", g=2, h=2)[:, :, h, :],
                           t["cache_k"][0, 0]).then_inc(cache_in, 16)
        pool.dma_start(V[:, 4, :], t["cache_v"][0, 0].rearrange("n g d -> n (g d)")).then_inc(cache_in, 16)
        pool.wait_ge(var_ok, 1)
        pow_mhalf(rstd[:], mv[:, :, 1], CH, 1.0).then_inc(rstd_ok, 1)
        for c in range(CH):
            pool.wait_ge(ss_ok, c + 1)
            pow_mhalf(rsq[:, c % 2, :], ssq[:, c % 2, :], 10, 1.0 / HD).then_inc(rs_ok, 1)
        pool.wait_ge(qr_ok, CH)
        pool.wait_ge(v_ok, CH)
        pool.dma_start(t["new_k"][0, 0].rearrange("n g d -> n (g d)"), qr[PC % 2][:, QW:QW + KVW]).then_inc(pool_out, 16)
        pool.dma_start(t["new_v"][0, 0].rearrange("n g d -> n (g d)"), V[:, 5, :]).then_inc(pool_out, 16)
        pool.wait_ge(qk_t, CH)
        pool.memset(BD[0:64, :, 64:128], 0.0).then_inc(bd_zero, 1)
        pool.memset(BD[64:128, :, 0:64], 0.0).then_inc(bd_zero, 1)
        for g, w in ((0, t["w_rg_a"]), (1, t["w_rg_x"])):
            for h in range(2):
                for d in range(2):
                    pool.dma_start(BD[64 * h:64 * h + 64, 8 * g + 4 * d:8 * g + 4 * d + 4, 64 * h:64 * h + 64],
                                   w[0, d, h::2].rearrange("j i o -> i j o")).then_inc(bd_in, 16)
        pool.wait_ge(r_ps, 8)
        link(pool.memset(b_row[:], 0.0))
        for gi, g in ((0, 2), (1, 5)):
            if gi == 1:
                pool.wait_ge(gate_row, 1)
            for row in (0, 32):
                pool.dma_start(b_row[row:row + 1, :], t["b_mod"][:, g * D:(g + 1) * D]).then_inc(brow_in, 16)
            pool.wait_ge(gate_row, gi + 1)
            for s, row in ((0, 0), (1, 32)):
                pool.dma_start(gates_dram[gi, s:s + 1, :], m_row[row:row + 1, :]).then_inc(gate_out, 16)
        pool.wait_ge(h_done, 2)
        for d, col in ((0, NT - 1), (1, N_S)):
            pool.dma_start(t["new_h"][0, 0, d].rearrange("(j p) -> p j", p=P), hst_out[:, d, :],
                           allow_slow_non_contiguous=True
                           ).then_inc(hout, 16)
        pool.wait_ge(rg_ok, 1)
        for c in range(CH):
            src = x_s[:, c, :] if c < PC else t["x_prompt"][0]
            pool.dma_start(xt[:, c, :], src).then_inc(x_again[c], 16)
        pool.wait_ge(cat_lo, 4)
        pool.wait_ge(cat_hi, 4)
        pool.wait_ge(gate_out, 64)
        pool.dma_start(G1[0][:], gates_dram[0, 0].partition_broadcast(P)).then_inc(g1_in, 16)
        pool.dma_start(G1[1][:], gates_dram[0, 1].partition_broadcast(P)).then_inc(g1_in, 16)
        pool.dma_start(ln1g[:], t["ln1_g"][0].partition_broadcast(P)).then_inc(g1_in, 16)
        pool.dma_start(ln1b[:], t["ln1_b"][0].partition_broadcast(P)).then_inc(g1_in, 16)
        for c in range(CH):
            for n in range(2):
                pool.wait_ge(var2_ok, 2 * c + n + 1)
                pow_mhalf(rstd[:, c:c + 1], mv[:, c, 1:2], 1, 1.0).then_inc(rstd2_ok, 1)
        pool.wait_ge(x2_lo, CH)
        pool.dma_start(G2[0:CAP_S, :], gates_dram[1, 0].partition_broadcast(CAP_S)).then_inc(g2_in, 16)
        pool.dma_start(G2[CAP_S:SL, :], gates_dram[1, 1].partition_broadcast(CAP_P)).then_inc(g2_in, 16)
        pool.wait_ge(X_lo, NE)
        pool.dma_start(ln2g[:], t["ln2_g"][0].partition_broadcast(P)).then_inc(ln2_in, 16)
        pool.dma_start(ln2b[:], t["ln2_b"][0].partition_broadcast(P)).then_inc(ln2_in, 16)
        for c in range(CH):
            pool.wait_ge(var3_ok, c + 1)
            pow_mhalf(rstd[:, c:c + 1], mv[:, c, 1:2], 1, 1.0).then_inc(rstd3_ok, 1)
        pool.wait_ge(pool_out, 32)
        pool.wait_ge(hout, 32)

    def pt_evac(act, u):
        h, c = u // CH, u % CH
        act.wait_ge(pt_ps, u + 1)
        if c == 0 and h:
            act.wait_ge(pv_ps, h)
        if c < PC:
            act.activation(PT[:, :, c * P:(c + 1) * P], PS[:, 2048:2048 + NT].rearrange("p (k n) -> p k n", k=5),
                           ACT.Copy).then_inc(pt_ok, 1)
        else:
            act.activation(PTp[:], PS[:, 2048:2048 + P], ACT.Copy).then_inc(pt_ok, 1)

    def cat_evac(act, j):
        act.wait_ge(pv_ps, 2 * j + 2)
        act.activation(Hh[:, j, :], PS[:, 3072:3072 + NT], ACT.Copy).then_inc(cat_hi, 1)

    @block.scalar
    def _(act):
        for c in range(CH):
            src = x_s[:, c, :] if c < PC else t["x_prompt"][0]
            act.dma_start(xt[:, c, :], src).then_inc(x_in[c], 16)
        act.wait_ge(nb_ok, 1)
        act.wait_ge(ct_zero, 1)
        act.activation(cT[:, :, 0], cols[:, R_C:R_C + 8], ACT.Silu).then_inc(ct_ok, 1)
        act.activation(cT[:, :, 32], cols[:, R_CTX:R_CTX + 8], ACT.Silu).then_inc(ct_ok, 1)
        act.activation(nsp[:, 2, :], lscr[:, 0, :], ACT.Exp, scale=-1.0).then_inc(lam_e, 1)
        for g in range(2):
            act.wait_ge(mod_used, KC * (g + 1))
            act.activation(m_rowA[g][:], PS[0:MG, 1024 * g:1024 * g + 1024], ACT.Copy).then_inc(mrow_ok, 1)

        def split_w(n, w):
            u = (U_Q + n // 2) if n < 16 else (U_O + (n - 16) // 2)
            landed_wait(act, u)
            if 8 <= n < 15:
                act.wait_ge(wa_used, n - 7)
            if n == 15:
                act.wait_ge(q_ps, CH)
            act.activation(WAh[:, n % 8, 0:w], ring[:, n % 8, 0:w], ACT.Copy).then_inc(split_hi, 1)

        act.wait_ge(modT_ok, 2)
        for k in range(KC):
            act.wait_ge(h_t, k + 1)
            if k >= 2:
                act.wait_ge(h_lo, k - 1)
            act.activation(hmod[k % 2][:, 0:N_S], bank(4 + 2 * (k % 2)), ACT.Identity,
                           bias=modT[:, 0, 0, k:k + 1], scale=modT[:, 1, 0, k:k + 1])
            act.activation(hmod[k % 2][:, N_S:NT], bank(5 + 2 * (k % 2), 0, N_P), ACT.Identity,
                           bias=modT[:, 0, 1, k:k + 1], scale=modT[:, 1, 1, k:k + 1]).then_inc(hmod_ok, 1)
            split_w(k, QKV)

        def qk_evac(c):
            act.wait_ge(qk_t, c + 1)
            o = c * P if c < PC else N_S
            act.activation(qT[:, :, o:o + P], bank(4).rearrange("p (j n) -> p j n", j=4), ACT.Copy)
            o = c * P if c < PC else N_S + PAST
            act.activation(kT[:, :, o:o + P], bank(5, 0, 256).rearrange("p (j n) -> p j n", j=2), ACT.Copy).then_inc(qk_ok, 1)

        for c in range(CH):
            if c == CH - 1:
                for n in range(8, 16):
                    split_w(n, 1024)
            act.wait_ge(q_ps, c + 1)
            b = 2 * (c % 2)
            if c >= 1:
                act.wait_ge(ss_ok, c)
            act.activation(sq[:, 0:QW], bank(b), ACT.Square)
            act.activation(sq[:, QW:QW + KVW], bank(b + 1, 0, KVW), ACT.Square).then_inc(sq_ok, 1)
            act.activation(V[:, c if c < PC else 5, :], bank(b + 1, KVW, 2 * KVW), ACT.Copy).then_inc(v_ok, 1)
            if c >= 2:
                qk_evac(c - 2)
        qk_evac(CH - 2)
        act.wait_ge(pads_ok, 1)
        for j in range(8):
            act.wait_ge(r_ps, j + 1)
            b = 2 * ((j + 1) % 2)
            if j < RJ:
                act.activation(xr[:, j, 2:2 + N_S], bank(b), ACT.Copy)
                act.activation(xr[:, j, 518:518 + N_P], bank(b + 1, 0, N_P), ACT.Copy).then_inc(r_ok, 1)
            else:
                act.activation(gel[:, j - RJ, 0:N_S], bank(b), ACT.Gelu_apprx_tanh)
                act.activation(gel[:, j - RJ, N_S:NT], bank(b + 1, 0, N_P), ACT.Gelu_apprx_tanh).then_inc(r_ok, 1)
            if j == 1:
                qk_evac(CH - 1)
                act.wait_ge(qk_t, CH + 1)
                act.activation(kT[:, :, N_S:N_S + PAST], bank(5, 0, 256).rearrange("p (j n) -> p j n", j=2),
                               ACT.Copy).then_inc(qk_ok, 1)
        for n in range(16):
            d, g, j = n // 8, (n // 4) % 2, n % 4
            act.wait_ge(g_ps, n + 1)
            b = 2 * ((n + 1) % 2)
            dst = (gate_r if g == 0 else gate_i)[d]
            bias = cols[:, (R_BA if g == 0 else R_BX) + 4 * d + j:(R_BA if g == 0 else R_BX) + 4 * d + j + 1]
            act.activation(dst[:, j, 0:N_S], bank(b), ACT.Sigmoid, bias=bias)
            act.activation(dst[:, j, N_S:NT], bank(b + 1, 0, N_P), ACT.Sigmoid, bias=bias).then_inc(g_ok, 1)
        act.wait_ge(nsp_ok, 1)
        act.wait_ge(g_ok, 16)
        for d in range(2):
            for j in range(RJ):
                act.activation(thx[d][:, j, :], gate_r[d][:, j, :], ACT.Tanh, scale=nsp[:, 1, 4 * d + j:4 * d + j + 1])
            for j in range(RJ):
                last = act.activation(gate_r[d][:, j, :], gate_r[d][:, j, :], ACT.Exp,
                                      scale=nsp[:, 0, 4 * d + j:4 * d + j + 1])
            last.then_inc(th_ok, 1)

        def mod_rows(g):
            act.wait_ge(mod_used, KC * (g + 1))
            act.wait_ge(gate_out, 32)
            if g == 4:
                act.wait_ge(mrow_t, 3)
            act.activation(m_row[:], PS[0:MG, 2048 + 1024 * (g % 2):3072 + 1024 * (g % 2)], ACT.Copy).then_inc(mrow_ok, 1)

        mod_rows(3)
        for d in range(2):
            act.wait_ge(om_ok, d + 1)
            act.activation(thx[d][:], thx[d][:], ACT.Sqrt).then_inc(sqr_ok, 1)
        mod_rows(4)

        act.wait_ge(rg_ok, 1)
        for u in range(NQ * CH):
            h, c = u // CH, u % CH
            w = NT if c < PC else N_P
            act.wait_ge(nmax_ok, u + 1)
            if u >= 2:
                act.wait_ge(pt_ps, u - 1)
            act.activation(prob[u % 2][:, 0:w], PS[:, 1024 * (u % 2):1024 * (u % 2) + w], ACT.Exp,
                           bias=nmax[:, u % 2:u % 2 + 1], scale=SCALE, accum_out=ssum[:, u % 2:u % 2 + 1]).then_inc(exp_ok, 1)
            if u >= 1:
                pt_evac(act, u - 1)
            if c == 1 and h % 2 == 0 and h >= 2:
                cat_evac(act, h // 2 - 1)
            if c == 2:
                n = 16 + h
                landed_wait(act, U_O + h // 2)
                act.activation(WAh[:, h, :], ring[:, h, :], ACT.Copy).then_inc(split_hi, 1)
        pt_evac(act, NQ * CH - 1)
        cat_evac(act, 3)

        act.wait_ge(modT_ok, 4)
        for c in range(CH):
            act.wait_ge(xn2_ok, c + 1)
            act.activation(xt[:, c, :], xt[:, c, :], ACT.Copy, scale=ALPHA).then_inc(acc_ok, 1)
            act.wait_ge(x2_t, c + 1)
            if c:
                act.wait_ge(lg_ps, c)
            s = 0 if c < PC else 1
            for k in range(KC):
                last = act.activation(h2T[:, k, :], PS[:, 2048 + k * P:2048 + (k + 1) * P], ACT.Identity,
                                      bias=modT[:, 2, s, k:k + 1], scale=modT[:, 3, s, k:k + 1])
            last.then_inc(h2_ok, 1)
        act.wait_ge(lmax_ok, 1)
        act.activation(aff[:], aff[:], ACT.Exp).then_inc(lexp_ok, 1)
        act.wait_ge(out_ps, CH)
        for c in range(CH):
            act.activation(X2h[:, c, :], xn2[:, c, :], ACT.Copy).then_inc(x2_hi, 1)
        act.wait_ge(idxb_ps, 1)
        for n in range(3 * KC):
            k, part = n // 3, n % 3
            act.wait_ge(ga_ps, n + 1)
            b = 3 + n % 4
            s = 0 if part < 2 else 1
            dst = XS[:, 8 * part:8 * part + 8, k, 0:CAP_S] if part < 2 else XS[:, :, k, CAP_S:SL]
            src = (bank(b) if part < 2 else bank(b, 0, 256)).rearrange("p (e s) -> p e s", s=CAP_S if part < 2 else CAP_P)
            act.activation(dst, src, ACT.Identity, bias=modT[:, 2, s, k:k + 1],
                           scale=modT[:, 3, s, k:k + 1]).then_inc(ga_ok, 1)

        act.wait_ge(x2_lo, CH)
        act.wait_ge(ga_ok, 3 * KC)

        def y_split(b, n):
            act.wait_ge(y_ok, n)
            act.activation(Yh[b][:], ysc[:], ACT.Copy).then_inc(y_hi, 1)

        with act.Fori(0, NE // 2) as i:
            for b in range(2):
                act.activation(Xh[b][:], XS[:, 2 * i + b], ACT.Copy).then_inc(X_hi, 1)
                for q in range(E_PIECES):
                    n = E_PIECES * b + q
                    if q % 2 == 0:
                        act.wait_ge(landed[(q // 2) % 4], 192 * i + (16 * (UNITS_A // 4) + 32 * (3 * b + q // 8 + 1)))
                    act.wait_ge(W_used, PAIR_PIECES * i + (n + 1))
                    act.activation(Wh[:, n % WR, :], ring[:, n % RING, :], ACT.Copy).then_inc(W_hi, 1)
                    if q == 3:
                        y_split(1 - b, 2 * i + (b + 1))
                    if q in (11, 19):
                        h = (q - 11) // 8
                        act.wait_ge(W_used, PAIR_PIECES * i + (E_PIECES * b + 8 * h + 8 + WR))
                        act.activation(gate_act[h][:], bank(2 * h, rows=SL), ACT.Silu).then_inc(act_ok, 1)
                    if q in (16, 21):
                        h = 0 if q == 16 else 1
                        act.wait_ge(ht_ps, 4 * i + (2 * b + h + 1))
                        act.activation(HTh[:, 4 * h:4 * h + 4, :], bank(6, 0, 4 * SL).rearrange("p (k s) -> p k s", k=4),
                                       ACT.Copy).then_inc(ht_hi, 1)
        y_split(1, NE + 1)

    @block.tensor
    def _(pe):
        def three(out, w, x, first, last):
            pe.matmul(out, w[0], x[0], start=first, stop=False)
            pe.matmul(out, w[1], x[0], start=False, stop=False)
            return pe.matmul(out, w[0], x[1], start=False, stop=last)

        pe.wait_ge(rows_in, 16 * 9)
        pe.wait_ge(const_in, 16)
        pe.transpose(bank(7, 0, R_END), ring[0:R_END, 7, 0:P], ident[0:R_END, 0:R_END]).then_inc(rows_t, 1)

        def mod_group(g, u0):
            b = [0, 2, 4, 6, 4, 6][g]
            for k in range(KC):
                if k % 2 == 0:
                    landed_wait(pe, u0 + k // 2)
                for half in range(2):
                    last = pe.matmul(bank(b + half, rows=MG), cT[:, k, :],
                                     ring[:, k, 512 * half:512 * half + 512], start=(k == 0), stop=(k == KC - 1))
                last.then_inc(mod_used, 1)

        def row_transposes(src, b):
            for k in range(KC):
                last = pe.transpose(bank(b, MG * k, MG * k + MG), src[:, k * P:(k + 1) * P], ident[0:MG, 0:MG])
            last.then_inc(mrow_t, 1)

        pe.wait_ge(ct_ok, 2)
        mod_group(0, 0)
        mod_group(1, 4)
        for g in range(2):
            pe.wait_ge(mrow_ok, g + 1)
            row_transposes(m_rowA[g], 4 + g)
        pe.wait_ge(xn_ok, CH)
        pe.wait_ge(modT_ok, 2)
        for k in range(KC):
            if k >= 2:
                pe.wait_ge(hmod_ok, k - 1)
            for c in range(CH):
                b = (4 if c < PC else 5) + 2 * (k % 2)
                o = c * P if c < PC else 0
                last = pe.transpose(bank(b, o, o + P), xt[:, c, k * P:(k + 1) * P], ident)
            last.then_inc(h_t, 1)

        def qk_transposes(c):
            pe.wait_ge(qr_ok, c + 1)
            if c:
                pe.wait_ge(qk_ok, c)
            else:
                pe.wait_ge(hmod_ok, KC)
            for j in range(4):
                pe.transpose(bank(4, j * P, (j + 1) * P), qr[c % 2][:, j * P:(j + 1) * P], ident)
            for j in range(2):
                last = pe.transpose(bank(5, j * P, (j + 1) * P), kd[c % 2][:, j * P:(j + 1) * P], ident)
            last.then_inc(qk_t, 1)

        pe.wait_ge(mrow_ok, 2)
        for c in range(CH):
            b = 2 * (c % 2)
            if c >= 2:
                pe.wait_ge(q_free, c - 1)
                pe.wait_ge(v_ok, c - 1)
            for k in range(KC):
                if c == 0:
                    pe.wait_ge(h_lo, k + 1)
                    pe.wait_ge(split_lo, k + 1)
                x = (Hh[:, k, c * P:(c + 1) * P], Hl[:, k, c * P:(c + 1) * P])
                three(bank(b), x, (WAh[:, k, 0:QW], WAl[:, k, 0:QW]), k == 0, k == KC - 1)
                last = three(bank(b + 1, 0, 2 * KVW), x, (WAh[:, k, QW:QKV], WAl[:, k, QW:QKV]), k == 0, k == KC - 1)
                if c == CH - 1 and k < KC - 1:
                    last.then_inc(wa_used, 1)
            last.then_inc(q_ps, 1)
            if c >= 2:
                qk_transposes(c - 2)
        for j in range(8):
            b = 2 * ((j + 1) % 2)
            if j < 2:
                pe.wait_ge(q_free, CH - 1 + j)
                pe.wait_ge(v_ok, CH - 1 + j)
            else:
                pe.wait_ge(r_ok, j - 1)
            for k in range(KC):
                if j == 0:
                    pe.wait_ge(split_lo, 8 + k + 1)
                w = (WAh[:, k, j * P:(j + 1) * P], WAl[:, k, j * P:(j + 1) * P])
                three(bank(b), w, (Hh[:, k, 0:N_S], Hl[:, k, 0:N_S]), k == 0, k == KC - 1)
                last = three(bank(b + 1, 0, N_P), w, (Hh[:, k, N_S:NT], Hl[:, k, N_S:NT]), k == 0, k == KC - 1)
            last.then_inc(r_ps, 1)
            if j == 0:
                qk_transposes(CH - 2)
            if j == 1:
                qk_transposes(CH - 1)
                pe.wait_ge(qk_ok, CH)
                pe.wait_ge(cache_in, 48)
                for m in range(2):
                    last = pe.transpose(bank(5, m * P, (m + 1) * P), ckd[:, m * P:(m + 1) * P], ident)
                last.then_inc(qk_t, 1)
        pe.wait_ge(bd_zero, 2)
        pe.wait_ge(bd_in, 16 * 8)
        for n in range(16):
            d, g, j = n // 8, (n // 4) % 2, n % 4
            b = 2 * ((n + 1) % 2)
            if n < 2:
                pe.wait_ge(r_ok, 7 + n)
            else:
                pe.wait_ge(g_ok, n - 1)
            if n < 4:
                pe.wait_ge(xc_ok, j + 1)
            w = BD[:, 8 * g + 4 * d + j, :]
            pe.matmul(bank(b), w, XC[:, j, 0:N_S], start=True, stop=True)
            pe.matmul(bank(b + 1, 0, N_P), w, XC[:, j, N_S:NT], start=True, stop=True).then_inc(g_ps, 1)
        pe.wait_ge(qk_ok, CH + 1)
        mod_group(2, U_MB)
        mod_group(3, U_MB + 4)
        pe.wait_ge(gate_row, 1)
        mod_group(4, U_MB + 8)
        pe.wait_ge(mrow_ok, 3)
        pe.wait_ge(g_ok, 16)
        row_transposes(m_row, 0)
        mod_group(5, U_MB + 12)
        pe.wait_ge(mrow_ok, 4)
        row_transposes(m_row, 2)
        pe.wait_ge(modT_ok, 4)

        def scores(u):
            h, c = u // CH, u % CH
            rows = slice(64 * (h % 2), 64 * (h % 2) + 64)
            j, g, b = h // 2, h // (NQ // NKV), 2 * (u % 2)
            if u >= 2:
                pe.wait_ge(exp_ok, u - 1)
            if c < PC:
                q = qT[rows, j, c * P:(c + 1) * P]
                pe.matmul(bank(b), q, kT[rows, g, 0:N_S], start=True, stop=True)
                pe.matmul(bank(b + 1, 0, PAST), q, kT[rows, g, N_S:N_S + PAST], start=True, stop=True).then_inc(s_ps, 1)
            else:
                pe.matmul(bank(b, 0, N_P), qT[rows, j, N_S:NT], kT[rows, g, N_S + PAST:N_S + PAST + N_P],
                          start=True, stop=True).then_inc(s_ps, 1)

        scores(0)
        scores(1)
        for u in range(NQ * CH):
            h, c = u // CH, u % CH
            pe.wait_ge(prob_ok, u + 1)
            if u:
                pe.wait_ge(pt_ok, u)
            for k in range(5 if c < PC else 1):
                last = pe.transpose(PS[:, 2048 + k * P:2048 + (k + 1) * P], prob[u % 2][:, k * P:(k + 1) * P], ident)
            last.then_inc(pt_ps, 1)
            if u + 2 < NQ * CH:
                scores(u + 2)
            if c == CH - 1:
                pe.wait_ge(pt_ok, u + 1)
                if h == 0:
                    pe.wait_ge(gate_row, 2)
                elif h % 2 == 0:
                    pe.wait_ge(cat_lo, h // 2)
                g, r0 = h // (NQ // NKV), 64 * (h % 2)
                for k in range(5):
                    pe.matmul(PS[r0:r0 + 64, 3072:3584], V[:, k, g * HD:(g + 1) * HD], PT[:, k, :],
                              start=(k == 0), stop=(k == 4))
                pe.matmul(PS[r0:r0 + 64, 3584:3584 + N_P], V[:, 5, g * HD:(g + 1) * HD], PTp[:],
                          start=True, stop=True).then_inc(pv_ps, 1)

        def x2_transposes(c):
            pe.wait_ge(xn2_ok, c + 1)
            if c:
                pe.wait_ge(h2_ok, c)
            for k in range(KC):
                last = pe.transpose(PS[:, 2048 + k * P:2048 + (k + 1) * P], xn2[:, c, k * P:(k + 1) * P], ident)
            last.then_inc(x2_t, 1)

        def logits(c):
            pe.wait_ge(h2_ok, c + 1)
            for k in range(KC):
                last = pe.matmul(bank(6, c * NE, (c + 1) * NE), h2T[:, k, :], w_rt[:, k, :], start=(k == 0), stop=(k == KC - 1))
            last.then_inc(lg_ps, 1)

        pe.wait_ge(cat_lo, 4)
        pe.wait_ge(rg_ok, 1)
        pe.wait_ge(misc_in, 48)
        for c in range(CH):
            b = 2 * (c % 2)
            if c >= 2:
                pe.wait_ge(out_free, c - 1)
            for k in range(KC):
                if c == 0:
                    pe.wait_ge(split_lo, 16 + k + 1)
                x = (Hh[:, k, c * P:(c + 1) * P], Hl[:, k, c * P:(c + 1) * P])
                three(bank(b), x, (WAh[:, k, 0:512], WAl[:, k, 0:512]), k == 0, k == KC - 1)
                last = three(bank(b + 1), x, (WAh[:, k, 512:1024], WAl[:, k, 512:1024]), k == 0, k == KC - 1)
            last.then_inc(out_ps, 1)
            if c >= 2:
                x2_transposes(c - 2)
            if c >= 3:
                logits(c - 3)
        logits(CH - 3)
        for c in (CH - 2, CH - 1):
            x2_transposes(c)
            logits(c)
        pe.wait_ge(aff_ok, 1)
        for c in range(CH):
            out = PS[0:NE, 3584 + c * P:3584 + (c + 1) * P] if c < PC else PS[0:NE, 3072 + 256:3072 + 384]
            last = pe.transpose(out, aff[:, c, :], ident)
        last.then_inc(aff_t, 1)
        pe.wait_ge(idxx_ok, 1)
        pe.transpose(bank(7, 0, NE, rows=SL), topf[:], ident[0:NE, 0:NE])
        pe.transpose(bank(7, 16, 16 + NE, rows=SL), topv[:], ident[0:NE, 0:NE]).then_inc(top_t, 1)
        pe.wait_ge(ones_ok, 1)
        flat = idxx[:].rearrange("k e s -> k (e s)")
        pe.matmul(bank(0), ones16[:], flat[:, 0:512], start=True, stop=True)
        pe.matmul(bank(1), ones16[:], flat[:, 512:1024], start=True, stop=True)
        pe.matmul(bank(2, 0, 256), ones16[:], flat[:, 1024:1280], start=True, stop=True).then_inc(idxb_ps, 1)
        pe.wait_ge(S_ok, CH)
        pe.wait_ge(x2_lo, CH)
        for n in range(3 * KC):
            k, part = n // 3, n % 3
            b = 3 + n % 4
            if n >= 4:
                pe.wait_ge(ga_ok, n - 3)
            chunks = range(4) if part < 2 else (PC,)
            for c in chunks:
                sel = Ss[:, c, 8 * part:8 * part + 8, :] if part < 2 else Sp[:]
                out = (bank(b) if part < 2 else bank(b, 0, 256)).rearrange("p (e s) -> p e s", s=CAP_S if part < 2 else CAP_P)
                pe.matmul(out, X2h[:, c, k * P:(k + 1) * P], sel, start=(c == chunks[0]), stop=False)
                last = pe.matmul(out, X2l[:, c, k * P:(k + 1) * P], sel, start=False, stop=(c == chunks[-1]))
            last.then_inc(ga_ps, 1)

        pe.wait_ge(pre_ok, 2)
        pe.wait_ge(ga_ok, 3 * KC)
        for half in range(2):
            last = pe.matmul(bank(4 + half, rows=SL), zrow[:, 0:SL], zrow[:], start=True, stop=True)
        last.then_inc(W_used, WR)

        def combine(n, count):
            c, half = n // 2, n % 2
            pe.wait_ge(cb_free, count + 1)
            for b in range(2):
                lhs = ST[b][:, c * P:(c + 1) * P]
                pe.matmul(bank(7), lhs, Yh[b][:, 512 * half:512 * half + 512], start=(b == 0), stop=False)
                last = pe.matmul(bank(7), lhs, Yl[b][:, 512 * half:512 * half + 512], start=False, stop=(b == 1))
            last.then_inc(cb_ps, 1)

        with pe.Fori(0, NE // 2) as i:
            for b in range(2):
                for q in range(E_PIECES):
                    n = E_PIECES * b + q
                    s = n % WR
                    if q == 0:
                        pe.wait_ge(X_lo, 2 * i + (b + 1))
                    if q in (0, 8):
                        pe.wait_ge(hrow_ok, 4 * i + (2 * b + q // 8 + 1))
                    if q == 16:
                        pe.wait_ge(y_ok, 2 * i + (b + 1))
                    if q in (16, 20):
                        pe.wait_ge(ht_lo, 4 * i + (2 * b + (q - 16) // 4 + 1))
                    pe.wait_ge(W_lo, PAIR_PIECES * i + (n + 1))
                    k = q % 8
                    if q < 16:
                        x, o0 = (Xh[b][:, k, :], Xl[b][:, k, :]), 2 * (q // 8)
                    else:
                        x, o0 = (HTh[:, k, :], HTl[:, k, :]), 4
                    for half in range(2):
                        cs = slice(512 * half, 512 * half + 512)
                        last = three(bank(o0 + half, rows=SL), x, (Wh[:, s, cs], Wl[:, s, cs]), k == 0, k == 7)
                    last.then_inc(W_used, 1)
                    if q in (12, 17):
                        h = 0 if q == 12 else 1
                        pe.wait_ge(hrow_ok, 4 * i + (2 * b + h + 3))
                        if h == 1:
                            pe.wait_ge(ht_lo, 4 * i + (2 * b + 1))
                        for m in range(4):
                            last = pe.transpose(bank(6, m * SL, (m + 1) * SL), hrow[h][:, m * P:(m + 1) * P],
                                                ident[0:SL, 0:SL])
                        last.then_inc(ht_ps, 1)
                    if b == 0 and 6 <= q < 16:
                        if q == 6:
                            pe.wait_ge(y_lo, 2 * i + 1)
                        combine(q - 6, 10 * i + (q - 6))
        pe.wait_ge(y_lo, NE + 1)
        for n in range(10):
            combine(n, 5 * NE + n)

    @block.vector
    def _(dve):
        seq = [0]

        def link(ins):
            seq[0] += 1
            ins.then_inc(dve_seq, 1)
            dve.wait_ge(dve_seq, seq[0])

        def layer_stats(src, c):
            for h in range(2):
                last = dve.bn_stats(stats[:, c, h, :], src[:, 512 * h:512 * h + 512])
            link(last)
            return dve.bn_aggr(mv[:, c, :], stats[:, c])

        dve.memset(ones16[:], 1.0).then_inc(ones_ok, 1)
        dve.wait_ge(rows_t, 1)
        link(dve.tensor_copy(cols[:], bank(7, 0, R_END)))
        link(dve.tensor_scalar(lscr[:, 1, :], cols[:, R_LAM:R_LAM + 8], -1.0, None, ALU.mult))
        dve.tensor_tensor(lscr[:, 0, :], lscr[:, 1, :], cols[:, R_LAM:R_LAM + 8], ALU.max).then_inc(nb_ok, 1)
        for c in range(CH):
            dve.wait_ge(x_in[c], 16)
            last = layer_stats(xt[:, c, :], c)
        last.then_inc(var_ok, 1)
        dve.wait_ge(lam_e, 1)
        u, s, z, acc = nsp[:, 2, :], lscr[:, 2, :], lscr[:, 3, :], nsp[:, 1, :]
        link(dve.tensor_scalar(s, u, 2.0, None, ALU.add))
        link(dve.reciprocal(z, s))
        link(dve.tensor_tensor(s, u, z, ALU.mult))
        link(dve.tensor_tensor(z, s, s, ALU.mult))
        link(dve.tensor_scalar(acc, z, 1.0 / 19.0, None, ALU.mult))
        for m in (17, 15, 13, 11, 9, 7, 5, 3):
            link(dve.scalar_tensor_tensor(acc, acc, 1.0 / m, z, ALU.add, ALU.mult))
        link(dve.scalar_tensor_tensor(acc, acc, 1.0, s, ALU.add, ALU.mult))
        link(dve.tensor_scalar(z, lscr[:, 1, :], 0.0, C_LRU, ALU.max, ALU.mult))
        link(dve.scalar_tensor_tensor(acc, acc, 2.0 * C_LRU, z, ALU.mult, ALU.add))
        dve.tensor_scalar(nsp[:, 0, :], acc, -1.0, None, ALU.mult).then_inc(nsp_ok, 1)

        dve.wait_ge(rstd_ok, 1)
        for c in range(CH):
            dve.tensor_scalar(xt[:, c, :], xt[:, c, :], mv[:, c, 0:1], rstd[:, c:c + 1],
                              ALU.subtract, ALU.mult).then_inc(xn_ok, 1)

        def mod_cols(g, b, w, plus):
            dve.wait_ge(mrow_t, {0: 1, 1: 2, 3: 3, 4: 4}[g])
            src = bank(b, 0, MG * KC).rearrange("p (k m) -> p k m", m=MG)
            for s_ in range(2):
                last = dve.scalar_tensor_tensor(modT[:, w, s_, :], src[:, :, 32 * s_], plus,
                                                cols[:, R_BM + 8 * g:R_BM + 8 * g + 8], ALU.add, ALU.add)
            last.then_inc(modT_ok, 1)

        mod_cols(0, 4, 0, 0.0)
        mod_cols(1, 5, 1, 1.0)

        def split_lo_w(n, w):
            dve.wait_ge(split_hi, n + 1)
            dve.tensor_tensor(WAl[:, n % 8, 0:w], ring[:, n % 8, 0:w], WAh[:, n % 8, 0:w].bitcast(F32),
                              ALU.subtract).then_inc(split_lo, 1)

        for k in range(KC):
            dve.wait_ge(hmod_ok, k + 1)
            link(dve.tensor_copy(Hh[:, k, :], hmod[k % 2][:]))
            dve.tensor_tensor(Hl[:, k, :], hmod[k % 2][:], Hh[:, k, :].bitcast(F32), ALU.subtract).then_inc(h_lo, 1)
            split_lo_w(k, QKV)

        dve.wait_ge(h_t, KC)
        dve.memset(xr[:, :, 0:2], 0.0)
        dve.memset(xr[:, :, 514:518], 0.0)
        dve.memset(xr[:, :, 646:648], 0.0).then_inc(pads_ok, 1)

        def heads(ap, n):
            return ap.rearrange("p (h d) -> p h d", h=n)

        def pairs(ap):
            return ap.rearrange("p (h a b n) -> p h a b n", h=10, a=2, b=2)

        for c in range(CH):
            b = 2 * (c % 2)
            dve.wait_ge(sq_ok, c + 1)
            dve.tensor_reduce(ssq[:, c % 2, :], heads(sq[:], 10), AX.X, ALU.add).then_inc(ss_ok, 1)
            if c == 0:
                dve.wait_ge(misc_in, 48)
            dve.wait_ge(rs_ok, c + 1)
            dve.wait_ge(v_ok, c + 1)
            dve.tensor_tensor(heads(qn[:, 0:QW], 8), heads(bank(b), 8),
                              rsq[:, c % 2, 0:8].unsqueeze(2).broadcast_to([P, 8, HD]), ALU.mult)
            last = dve.tensor_tensor(heads(qn[:, QW:640], 2), heads(bank(b + 1, 0, KVW), 2),
                                     rsq[:, c % 2, 8:10].unsqueeze(2).broadcast_to([P, 2, HD]), ALU.mult)
            last.then_inc(q_free, 1)
            dve.wait_ge(q_free, c + 1)
            dst = qn if c < PC else qr[c % 2]
            if c >= 2:
                dve.wait_ge(qk_t, c - 1)
            dve.tensor_tensor(heads(dst[:, 0:QW], 8), heads(qn[:, 0:QW], 8),
                              gqk[:, 0, :].unsqueeze(1).broadcast_to([P, 8, HD]), ALU.mult)
            link(dve.tensor_tensor(heads(dst[:, QW:640], 2), heads(qn[:, QW:640], 2),
                                   gqk[:, 1, :].unsqueeze(1).broadcast_to([P, 2, HD]), ALU.mult))
            if c < PC:
                def cs(w):
                    return rope[:, c, w, :].rearrange("p (a n) -> p a n", a=2).unsqueeze(1).broadcast_to([P, 10, 2, 16])
                x1, x2 = pairs(qn[:])[:, :, :, 0, :], pairs(qn[:])[:, :, :, 1, :]
                y1, y2 = pairs(qr[c % 2][:])[:, :, :, 0, :], pairs(qr[c % 2][:])[:, :, :, 1, :]
                t1 = rt[:, 0, :].rearrange("p (h a n) -> p h a n", h=10, a=2)
                t2 = rt[:, 1, :].rearrange("p (h a n) -> p h a n", h=10, a=2)
                dve.tensor_tensor(t1, x1, cs(0), ALU.mult)
                link(dve.tensor_tensor(t2, x2, cs(1), ALU.mult))
                link(dve.tensor_tensor(y1, t1, t2, ALU.subtract))
                dve.tensor_tensor(t1, x1, cs(1), ALU.mult)
                link(dve.tensor_tensor(t2, x2, cs(0), ALU.mult))
                link(dve.tensor_tensor(y2, t1, t2, ALU.add))
            dve.tensor_copy(kd[c % 2][:].rearrange("p (g h d) -> p g h d", g=2, h=2),
                            heads(qr[c % 2][:, QW:640], 2).unsqueeze(2).broadcast_to([P, 2, 2, HD])).then_inc(qr_ok, 1)
            if c == CH - 2:
                for n in range(8, 16):
                    split_lo_w(n, 1024)

        dve.wait_ge(qk_t, CH + 1)
        dve.wait_ge(pool_out, 32)
        for j in range(RJ):
            dve.wait_ge(r_ok, j + 1)
            for o0, i0, w in ((0, 0, N_S), (N_S, 516, N_P)):
                def tap(m):
                    return xr[:, j, i0 + m:i0 + m + w]
                cw = [cols[:, R_CW + 4 * m + j:R_CW + 4 * m + j + 1] for m in range(4)]
                out = XC[:, j, o0:o0 + w]
                link(dve.tensor_scalar(out, tap(0), cw[0], cols[:, R_CB + j:R_CB + j + 1], ALU.mult, ALU.add))
                for m in (1, 2):
                    link(dve.scalar_tensor_tensor(out, tap(m), cw[m], out, ALU.mult, ALU.add))
                last = dve.scalar_tensor_tensor(out, tap(3), cw[3], out, ALU.mult, ALU.add)
            last.then_inc(xc_ok, 1)

        def gate_rows(gi):
            g = (2, 5)[gi]
            dve.wait_ge(mod_used, KC * (g + 1))
            dve.wait_ge(brow_in, 32 * (gi + 1))
            if gi == 1:
                dve.wait_ge(mrow_t, 4)
            dve.tensor_tensor(m_row[:], PS[0:MG, 2048 + 1024 * gi:3072 + 1024 * gi], b_row[:], ALU.add).then_inc(gate_row, 1)

        dve.wait_ge(xc_ok, RJ)
        for d in range(2):
            dve.wait_ge(g_ok, 8 * (d + 1))
            link(dve.tensor_tensor(gate_i[d][:], gate_i[d][:], XC[:], ALU.mult))
        for d in range(2):
            dve.wait_ge(th_ok, d + 1)
            link(dve.tensor_tensor(hst[d][:], gate_r[d][:], gate_r[d][:], ALU.mult))
            dve.scalar_tensor_tensor(thx[d][:].rearrange("p j n -> p (j n)"), hst[d][:].rearrange("p j n -> p (j n)"), 1.0,
                                     thx[d][:].rearrange("p j n -> p (j n)"), ALU.add, ALU.mult).then_inc(om_ok, 1)
        gate_rows(0)
        for d in range(2):
            dve.wait_ge(sqr_ok, d + 1)
            link(dve.tensor_tensor(gate_i[d][:], thx[d][:], gate_i[d][:], ALU.mult))
            for j in range(RJ):
                h0 = cols[:, R_H0 + 4 * d + j:R_H0 + 4 * d + j + 1]
                for o0, w, init in ((0, N_S, h0), (N_S, N_P, 0.0)):
                    a_, b_, h_ = (x_[:, j, o0:o0 + w] for x_ in (gate_r[d], gate_i[d], hst[d]))
                    if d:
                        a_, b_, h_ = a_[:, ::-1], b_[:, ::-1], h_[:, ::-1]
                    last = dve.tensor_tensor_scan(h_, a_, b_, init, ALU.mult, ALU.add)
            link(last)
            col = NT - 1 if d == 0 else N_S
            dve.tensor_copy(hst_out[:, d, :], hst[d][:, :, col]).then_inc(h_done, 1)
            if d == 0:
                mod_cols(3, 0, 2, 0.0)
        link(dve.tensor_tensor(hst[0][:], hst[0][:], hst[1][:], ALU.add))
        link(dve.tensor_tensor(hst[0][:], hst[0][:], gel[:], ALU.mult))
        link(dve.tensor_copy(Hh[:, 4:8, :], hst[0][:]))
        dve.tensor_tensor(Hl[:, 4:8, :], hst[0][:], Hh[:, 4:8, :].bitcast(F32), ALU.subtract).then_inc(rg_ok, 1)
        mod_cols(4, 2, 3, 1.0)
        gate_rows(1)

        def cat_lo_evac(j):
            dve.wait_ge(cat_hi, j + 1)
            dve.tensor_tensor(Hl[:, j, :], PS[:, 3072:3072 + NT], Hh[:, j, :].bitcast(F32), ALU.subtract).then_inc(cat_lo, 1)

        for u in range(NQ * CH + 1):
            h, c = u // CH, u % CH
            if u < NQ * CH:
                w = NT if c < PC else N_P
                dve.wait_ge(s_ps, u + 1)
                if u >= 2:
                    dve.wait_ge(exp_ok, u - 1)
                link(dve.tensor_reduce(smax[:, u % 2:u % 2 + 1], PS[:, 1024 * (u % 2):1024 * (u % 2) + w], AX.X, ALU.max))
                dve.tensor_scalar(nmax[:, u % 2:u % 2 + 1], smax[:, u % 2:u % 2 + 1], -SCALE, None, ALU.mult).then_inc(nmax_ok, 1)
            if u:
                v = u - 1
                w = NT if v % CH < PC else N_P
                dve.wait_ge(exp_ok, u)
                link(dve.reciprocal(rsum[:, v % 2:v % 2 + 1], ssum[:, v % 2:v % 2 + 1]))
                dve.tensor_scalar(prob[v % 2][:, 0:w], prob[v % 2][:, 0:w], rsum[:, v % 2:v % 2 + 1], None,
                                  ALU.mult).then_inc(prob_ok, 1)
            if u < NQ * CH and c == 2 and h % 2 == 0 and h >= 2:
                cat_lo_evac(h // 2 - 1)
            if u < NQ * CH and c == 3:
                dve.wait_ge(split_hi, 16 + h + 1)
                dve.wait_ge(gate_out, 64)
                dve.tensor_tensor(WAl[:, h, :], ring[:, h, :], WAh[:, h, :].bitcast(F32), ALU.subtract).then_inc(split_lo, 1)
        cat_lo_evac(3)

        def norm(dst, src, c):
            return dve.tensor_scalar(dst, src, mv[:, c, 0:1], rstd[:, c:c + 1], ALU.subtract, ALU.mult)

        dve.wait_ge(g1_in, 64)
        for c in range(CH):
            s_ = 0 if c < PC else 1
            x = xt[:, c, :]
            dve.wait_ge(out_ps, c + 1)
            dve.wait_ge(x_again[c], 16)
            link(dve.tensor_tensor(xn2[:, c, :], PS[:, 1024 * (c % 2):1024 * (c % 2) + 1024], G1[s_][:], ALU.mult))
            dve.scalar_tensor_tensor(x, x, ALPHA, xn2[:, c, :], ALU.mult, ALU.add).then_inc(out_free, 1)
            dve.wait_ge(out_free, c + 1)
            layer_stats(x, c).then_inc(var2_ok, 1)
            dve.wait_ge(rstd2_ok, 2 * c + 1)
            link(norm(x, x, c))
            link(dve.tensor_tensor(x, x, ln1g[:], ALU.mult))
            link(dve.tensor_tensor(x, x, ln1b[:], ALU.add))
            layer_stats(x, c).then_inc(var2_ok, 1)
            dve.wait_ge(rstd2_ok, 2 * c + 2)
            norm(xn2[:, c, :], x, c).then_inc(xn2_ok, 1)
        dve.wait_ge(lg_ps, CH)
        lg = bank(6, 0, CH * NE).rearrange("p (c e) -> p c e", c=CH)
        link(dve.tensor_reduce(rmax[:], lg, AX.X, ALU.max))
        dve.tensor_tensor(aff[:], lg, rmax[:].unsqueeze(2).broadcast_to([P, CH, NE]), ALU.subtract).then_inc(lmax_ok, 1)
        dve.wait_ge(lexp_ok, 1)
        link(dve.tensor_reduce(rmax[:], aff[:], AX.X, ALU.add))
        link(dve.reciprocal(rmax[:], rmax[:]))
        dve.tensor_tensor(aff[:], aff[:], rmax[:].unsqueeze(2).broadcast_to([P, CH, NE]), ALU.mult).then_inc(aff_ok, 1)
        dve.wait_ge(aff_t, 1)
        dve.wait_ge(out_ps, CH)
        dve.tensor_copy(affw[:, 0:N_S], PS[0:NE, 3584:4096])
        link(dve.tensor_copy(affw[:, N_S:NT], PS[0:NE, 3072 + 256:3072 + 384]))
        for a0, w, v0, cap in ((0, N_S, 0, CAP_S), (N_S, N_P, CAP_S, CAP_P)):
            vals = affw[:, a0:a0 + w]
            for r in range(cap // 8):
                tv = topv[:, v0 + 8 * r:v0 + 8 * r + 8]
                link(dve.max(tv, vals))
                link(dve.max_index(topi[:, v0 + 8 * r:v0 + 8 * r + 8], tv, vals))
                link(dve.match_replace(vals, tv, vals, -1.0))
        dve.tensor_copy(topf[:, 0:CAP_S], topi[:, 0:CAP_S])
        link(dve.tensor_scalar(topf[:, CAP_S:SL], topi[:, CAP_S:SL], float(N_S), None, ALU.add))
        dve.tensor_tensor(idxx[:], topf[:].unsqueeze(1).broadcast_to([NE, NE, SL]),
                          ident[0:NE, 0:NE].unsqueeze(2).broadcast_to([NE, NE, SL]), ALU.mult).then_inc(idxx_ok, 1)
        for c in range(CH):
            dve.wait_ge(x2_hi, c + 1)
            dve.tensor_tensor(X2l[:, c, :], xn2[:, c, :], X2h[:, c, :].bitcast(F32), ALU.subtract).then_inc(x2_lo, 1)
        dve.wait_ge(top_t, 1)
        dve.memset(idx_slot[:, 0:1], -1.0)
        dve.memset(g_slot[:, 0:1], 0.0)
        dve.tensor_copy(idx_slot[:, 1:NE + 1], bank(7, 0, NE, rows=SL))
        dve.tensor_copy(g_slot[:, 1:NE + 1], bank(7, 16, 16 + NE, rows=SL)).then_inc(slot_ok, 1)
        dve.wait_ge(idxb_ps, 1)
        ib = PS[:, 0:NE * SL].rearrange("p (e s) -> p e s", e=NE)
        for c in range(CH):
            dst, src = (Ss[:, c], ib[:, :, 0:CAP_S]) if c < PC else (Sp[:], ib[:, :, CAP_S:SL])
            dve.tensor_scalar(dst, src, tok_id[:, c:c + 1], None, ALU.is_equal).then_inc(S_ok, 1)

        dve.wait_ge(ga_ps, 3 * KC)
        dve.memset(zrow[:], 0.0).then_inc(hrow_ok, 2)
        dve.memset(Yh[0][:].bitcast(F32), 0.0).then_inc(cb_free, 1)
        dve.memset(Yl[0][:].bitcast(F32), 0.0)
        dve.memset(ST[0][:].bitcast(F32), 0.0).then_inc(pre_ok, 2)
        dve.wait_ge(slot_ok, 1)
        dve.wait_ge(g2_in, 32)
        dve.wait_ge(acc_ok, CH)

        def y_evac(b, count, e1, used):
            dve.wait_ge(W_used, used)
            dve.scalar_tensor_tensor(ysc[:], PS[0:SL, 2048:3072], g_slot[:, e1], G2[:], ALU.mult, ALU.mult).then_inc(y_ok, 1)
            dve.tensor_scalar(ST[b][:], iota_tok[0:SL, :], idx_slot[:, e1], None, ALU.is_equal)
            dve.wait_ge(y_hi, count)
            dve.tensor_tensor(Yl[b][:], ysc[:], Yh[b][:].bitcast(F32), ALU.subtract).then_inc(y_lo, 1)

        def add_group(n, count):
            c, half = n // 2, n % 2
            dve.wait_ge(cb_ps, count)
            dst = xt[:, c, 512 * half:512 * half + 512]
            return dve.tensor_tensor(dst, dst, bank(7), ALU.add).then_inc(cb_free, 1)

        with dve.Fori(0, NE // 2) as i:
            for b in range(2):
                dve.wait_ge(X_hi, 2 * i + (b + 1))
                dve.tensor_tensor(Xl[b][:], XS[:, 2 * i + b], Xh[b][:].bitcast(F32), ALU.subtract).then_inc(X_lo, 1)
                for q in range(E_PIECES):
                    n = E_PIECES * b + q
                    dve.wait_ge(W_hi, PAIR_PIECES * i + (n + 1))
                    dve.tensor_tensor(Wl[:, n % WR, :], ring[:, n % RING, :], Wh[:, n % WR, :].bitcast(F32),
                                      ALU.subtract).then_inc(W_lo, 1)
                    if q == 3:
                        y_evac(1 - b, 2 * i + (b + 1), bass.ds(2 * i + b, 1), PAIR_PIECES * i + (E_PIECES * b + WR))
                    if q in (11, 19):
                        h = (q - 11) // 8
                        dve.wait_ge(act_ok, 4 * i + (2 * b + h + 1))
                        dve.tensor_tensor(hrow[h][:], gate_act[h][:], bank(2 * h + 1, rows=SL), ALU.mult).then_inc(hrow_ok, 1)
                    if q in (16, 21):
                        h = 0 if q == 16 else 1
                        dve.wait_ge(ht_hi, 4 * i + (2 * b + h + 1))
                        dve.tensor_tensor(HTl[:, 4 * h:4 * h + 4, :], bank(6, 0, 4 * SL).rearrange("p (k s) -> p k s", k=4),
                                          HTh[:, 4 * h:4 * h + 4, :].bitcast(F32), ALU.subtract).then_inc(ht_lo, 1)
                    if b == 0 and 8 <= q < 18:
                        add_group(q - 8, 10 * i + (q - 8 + 1))
        y_evac(1, NE + 1, slice(NE, NE + 1), NE * E_PIECES + WR)

        for c in range(CH):
            x = xt[:, c, :]
            add_group(2 * c, 5 * NE + 2 * c + 1)
            add_group(2 * c + 1, 5 * NE + 2 * c + 2)
            dve.wait_ge(cb_free, 5 * NE + 2 * c + 3)
            layer_stats(x, c).then_inc(var3_ok, 1)
            dve.wait_ge(rstd3_ok, c + 1)
            link(norm(x, x, c))
            if c == 0:
                dve.wait_ge(ln2_in, 32)
            link(dve.tensor_tensor(x, x, ln2g[:], ALU.mult))
            if c >= 2:
                dve.wait_ge(stored[c % 2], 16 * (c // 2))
            dve.tensor_tensor(osb[:, c % 2, :], x, ln2b[:], ALU.add).then_inc(y_out, 1)


_INS = ["x_prompt", "x_sample", "cache_k", "cache_v", "state_h", "c", "c_ctx", "w_mod", "b_mod", "w_in", "q_norm_g",
        "k_norm_g", "conv_w", "conv_b", "w_rg_a", "b_rg_a", "w_rg_x", "b_rg_x", "rg_lambda", "w_out", "ln1_g", "ln1_b",
        "w_router", "w_gate_up", "w_down", "ln2_g", "ln2_b"]
_OUTS = [("y_prompt", (1, N_P, D)), ("y_sample", (1, N_S, D)), ("new_k", (1, 1, N_P, NKV, HD)),
         ("new_v", (1, 1, N_P, NKV, HD)), ("new_h", (1, 1, 2, RG))]


def shape_constants():
    out = np.zeros((P, P + 256 + NT + CH), np.float32)
    out[:, 0:P] = np.eye(P)
    nf = HD // 4
    inv = 10000.0 ** (-np.arange(nf) / nf)
    tok = np.arange(N_S)
    ang = np.concatenate([(tok // GRID_W)[:, None] * inv, (tok % GRID_W)[:, None] * inv], axis=1)
    cs = np.stack([np.cos(ang), np.sin(ang)], axis=1).reshape(4, P, 2, 2 * nf)
    out[:, P:P + 256] = cs.transpose(1, 0, 2, 3).reshape(P, 256)
    out[:, P + 256:P + 256 + NT] = np.arange(NT)
    out[:, P + 256 + NT:] = np.arange(P)[:, None] + P * np.arange(CH)[None, :]
    return out


def kernel(**inputs):
    import concourse.bacc as bacc
    from concourse.bass_utils import run_bass_kernel_spmd

    nc = bacc.Bacc("TRN2", target_bir_lowering=False, num_devices=1)
    arrays, t = {}, {}
    for name in _INS + ["consts"]:
        a = shape_constants() if name == "consts" else np.ascontiguousarray(inputs[name])
        arrays[f"in_{name}"] = a
        t[name] = nc.dram_tensor(f"in_{name}", a.shape, mybir.dt.from_np(a.dtype), kind="ExternalInput").ap()
    for name, shape in _OUTS:
        t[name] = nc.dram_tensor(f"out_{name}", shape, F32, kind="ExternalOutput").ap()
    build(nc, t)
    r = run_bass_kernel_spmd(nc, [arrays], core_ids=[0])
    return tuple(r.results[0][f"out_{name}"] for name, _ in _OUTS)
```

```python
from contextlib import ExitStack

import numpy as np

import concourse.bass as bass
from concourse import mybir

F32 = mybir.dt.float32
F32R = mybir.dt.float32r
U32 = mybir.dt.uint32
ALU = mybir.AluOpType
ACT = mybir.ActivationFunctionType
AX = mybir.AxisListType

P = 128
D = 1024
KC = D // P
N_S, N_P = 512, 128
NT = N_S + N_P
HN = NT // 2
CH = NT // P
PC = CH - 1
PAST = 128
HD, NQ, NKV = 64, 8, 2
QW, KVW = NQ * HD, NKV * HD
QKV = QW + 2 * KVW
RG = 512
RJ = RG // P
NE, CAP_S, CAP_P = 16, 64, 16
SL = CAP_S + CAP_P
EPS = 1e-6
ALPHA = 2.0 ** 0.25
SCALE = HD ** -0.5
C_LRU = 8.0
MG = 33
GRID_W = 64

RING = 8
WR = 8
EB = 4
E_PIECES = 3 * KC
BODY_PIECES = EB * E_PIECES
X_STEP, A_STEP, T_STEP, Y_STEP = (7, 11), (12, 20), (16, 22), 4
PX_STEP, PT_STEP = (2, 6), (11, 18)
CB_START, CB_EVERY, CB_LAG = 7, 4, 4
RG_UNITS, W_UNITS = (9, 10, 14, 15), (19, 20, 24, 25, 29, 30, 34, 35)
POOL_LAST = 3
UNITS_A = (16 + 8 + 24 + 8 + 8) // 2

R_C, R_CTX, R_BM, R_CW, R_CB, R_BA, R_BX, R_LAM, R_H0, R_END = 0, 8, 16, 64, 80, 84, 92, 100, 108, 116


def build(nc, t):
    with ExitStack() as ctx:
        _build(nc, ctx, t)


def _build(nc, ctx, t):
    def sem(name):
        return ctx.enter_context(nc.semaphore(name))

    base = -(-nc.sbuf_base // 64) * 64
    RAW = nc.sbuf_usable_end - 200960 - 64
    RAW -= RAW % 64
    Bz, Cz = RAW, RAW + 32768
    Dz = Cz + 20736
    Ez = Dz + 65536
    Fz = Ez + 40960
    assert Fz + 40960 <= nc.sbuf_usable_end
    small = [base]

    def at(name, shape, off, dt=F32):
        return nc.alloc_sbuf_tensor_at(name, shape, dt, offset=off)

    def tile(name, shape, dt=F32):
        n = 4
        for s in shape[1:]:
            n *= s
        off = small[0]
        small[0] += -(-n // 32) * 32
        assert small[0] <= RAW, (name, small[0], RAW)
        return at(name, shape, off, dt)

    consts = tile("consts", [P, P + 256 + NT])
    ident = consts[:, 0:P]
    rope = consts[:, P:P + 256].rearrange("p (c w n) -> p c w n", c=4, w=2)
    iota_tok = consts[:, P + 256:P + 256 + NT]
    cols = tile("cols", [P, R_END])
    cT = tile("cT", [P, KC, MG])
    modT = tile("modT", [P, 2, 2, KC])
    stats = tile("stats", [P, CH, 2, 6])
    mv = tile("mv", [P, CH, 2])
    rstd = tile("rstd", [P, CH])
    nmr = tile("nmr", [P, CH])
    ptmp = tile("ptmp", [P, 16])
    mhalf = tile("mhalf", [P, 16])
    ssq = tile("ssq", [P, 2, 10])
    rsq = tile("rsq", [P, 2, 10])
    gqk = tile("gqk", [P, 2, HD])
    w_rt = tile("w_rt", [P, KC, NE])
    nsp = tile("nsp", [P, 3, 8])
    lscr = tile("lscr", [P, 4, 8])
    hst_out = tile("hst_out", [P, 2, RJ])
    smax = tile("smax", [P, 2])
    nmax = tile("nmax", [P, 2])
    ssum = tile("ssum", [P, 2])
    rsum = tile("rsum", [P, 2])
    rmax = tile("rmax", [P, CH])
    aff = tile("aff", [P, CH, NE])
    idx_slot = tile("idx_slot", [SL, NE + 1])
    g_slot = tile("g_slot", [SL, NE + 1])
    idx_u = tile("idx_u", [SL, NE + 1], U32)
    table_scr = tile("table_scr", [P, 1])
    wait_scr = tile("wait_scr", [P, 1])
    tok_now = tile("tok_now", [SL, 1])
    idx_now = [tile(f"idx_now{b}", [SL, 1], U32) for b in range(2)]
    topv = tile("topv", [NE, SL])
    topi = tile("topi", [NE, SL], U32)
    topf = tile("topf", [NE, SL])

    ring = at("ring", [P, RING, 1024], Bz)
    xt = at("xt", [P, CH, D], Cz)
    XRW = 648
    xr = at("xr", [P, RJ, XRW], Cz)
    gel = at("gel", [P, RJ, NT], Cz + 4 * RJ * XRW)
    WAh = at("WAh", [P, KC, 1024], Dz, F32R)
    WAl = at("WAl", [P, KC, 1024], Dz + 32768, F32R)
    w_qkv = at("w_qkv", [P, KC, 1024], Dz + 32768)
    B10 = 4 * RJ * NT
    gate_r = [at("gate_r0", [P, RJ, NT], Dz), at("gate_r1", [P, RJ, NT], Ez)]
    gate_i = [at("gate_i0", [P, RJ, NT], Dz + B10), at("gate_i1", [P, RJ, NT], Ez + B10)]
    thx = [at("thx0", [P, RJ, NT], Dz + 2 * B10), at("thx1", [P, RJ, NT], Ez + 2 * B10)]
    hst = [at("hst0", [P, RJ, NT], Dz + 3 * B10), at("hst1", [P, RJ, NT], Dz + 4 * B10)]
    b_row = at("b_row", [MG, D], Dz + 5 * B10)
    m_row = [at("m_row0", [MG, D], Dz + 5 * B10 + 4096), at("m_row1", [MG, D], Dz + 5 * B10 + 8192)]
    Hh = at("Hh", [P, KC, NT], Ez, F32R)
    Hl = at("Hl", [P, KC, NT], Ez + 20480, F32R)
    qT = at("qT", [P, 4, NT], Fz)
    kT = at("kT", [P, NKV, NT + PAST], Fz + 10240)
    V = at("V", [P, 6, KVW], Fz + 16384)
    Z = Fz + 19456
    m_rowA = [at("m_rowA0", [MG, D], Fz), at("m_rowA1", [MG, D], Fz + 4096)]
    hmod = [at("hmod0", [P, NT], Z), at("hmod1", [P, NT], Z + 2560)]
    sq = at("sq", [P, 640], Z + 5120)
    qn = at("qn", [P, 640], Z + 7680)
    qr = [at("qr0", [P, 640], Z + 10240), at("qr1", [P, 640], Z + 12800)]
    rt = at("rt", [P, 2, 320], Z + 15360)
    kd = [at("kd0", [P, 256], Z + 17920), at("kd1", [P, 256], Z + 18944)]
    ckd = at("ckd", [P, 256], Z + 19968)
    BD = at("BD", [P, 16, P], Z)
    XC = at("XC", [P, RJ, NT], Z + 8192)
    PT = at("PT", [P, 5, 512], Z + 5120)
    PTp = at("PTp", [P, P], Z + 15360)
    prob = [at("prob0", [P, 640], Z), at("prob1", [P, 640], Z + 2560), at("prob2", [P, 640], Z + 15872)]
    h2 = [at("h2_0", [P, D], Fz), at("h2_1", [P, D], Fz + 4096)]
    h2T = at("h2T", [P, KC, P], Fz + 8192)
    G1 = [at("G1s", [P, D], Fz + 12288), at("G1p", [P, D], Fz + 16384)]
    ln1g = at("ln1g", [P, D], Fz + 20480)
    ln1b = at("ln1b", [P, D], Fz + 24576)
    sc2 = [at("sc2s", [P, D], Fz + 28672), at("sc2p", [P, D], Fz + 12288)]
    sh2 = [at("sh2s", [P, D], Fz + 32768), at("sh2p", [P, D], Fz + 36864)]
    affw = at("affw", [NE, NT], Ez)
    b5_row = at("b5_row", [MG, D], Fz + 36864)
    m5_row = at("m5_row", [MG, D], Fz + 32768)
    Xg = [at("Xg0", [SL, D], Ez), at("Xg1", [SL, D], Ez + 4096)]
    Wl = at("Wl", [P, WR, 1024], Ez + 8192, F32R)
    Wh = at("Wh", [P, WR, 1024], Fz, F32R)
    G2 = at("G2", [SL, D], Fz + 32768)
    ysc = at("ysc", [SL, D], Fz + 36864)
    o = Dz
    Xh, Xl, Yh, Yl, ST = [], [], [], [], []
    for b in range(2):
        Xh.append(at(f"Xh{b}", [P, KC, SL], o, F32R)); o += 4 * KC * SL
        Xl.append(at(f"Xl{b}", [P, KC, SL], o, F32R)); o += 4 * KC * SL
    for b in range(EB):
        Yh.append(at(f"Yh{b}", [SL, D], o, F32R)); o += 4096
        Yl.append(at(f"Yl{b}", [SL, D], o, F32R)); o += 4096
        ST.append(at(f"ST{b}", [SL, NT], o, F32R)); o += 2560
    gate_act = at("gate_act", [SL, 512], o); o += 2048
    hrow = at("hrow", [SL, 512], o); o += 2048
    HTh = at("HTh", [P, KC, SL], o, F32R); o += 4 * KC * SL
    HTl = at("HTl", [P, KC, SL], o, F32R); o += 4 * KC * SL
    assert o <= Dz + 65536
    ln2g = at("ln2g", [P, D], Ez)
    ln2b = at("ln2b", [P, D], Ez + 4096)

    PS = ctx.enter_context(nc.psum_tensor("PS", [P, 4096], F32))

    def bank(b, lo=0, hi=512, rows=P):
        return PS[0:rows, 512 * b + lo:512 * b + hi]

    rt_w = t["w_router"][0].rearrange("(k p) e -> p k e", p=P)
    w_mod_v = t["w_mod"][0].rearrange("(k p) (g n) -> p k g n", p=P, n=D)
    w_in_v = t["w_in"][0].rearrange("(k p) n -> p k n", p=P)
    w_out_v = t["w_out"][0].rearrange("(k p) n -> p k n", p=P)
    w_gu_v = t["w_gate_up"][0].rearrange("e (k p) (g h n) -> e p k g h n", p=P, g=2, h=2)
    w_dn_v = t["w_down"][0].rearrange("e (k p) n -> e p k n", p=P)
    mods_dram = nc.dram_tensor("mods_scratch", (4, 2, D), F32, kind="Internal").ap()
    h2_dram = nc.dram_tensor("h2_scratch", (NT, D), F32, kind="Internal").ap()
    y_s = t["y_sample"][0].rearrange("(c p) d -> p c d", p=P)
    x_s = t["x_sample"][0].rearrange("(c p) d -> p c d", p=P)

    rows_in, const_in, misc_in = sem("rows_in"), sem("const_in"), sem("misc_in")
    x_in = [sem(f"x_in{c}") for c in range(CH)]
    x_again = [sem(f"x_again{c}") for c in range(CH)]
    w_qkv_in = [sem(f"w_qkv_in{m}") for m in range(4)]
    landed = [sem(f"landed{s}") for s in range(RING // 2)]
    cache_in = sem("cache_in")
    rows_t, ct_zero, ct_ok = sem("rows_t"), sem("ct_zero"), sem("ct_ok")
    mod_used, mrow_ok, mrow_t, modT_ok = sem("mod_used"), sem("mrow_ok"), sem("mrow_t"), sem("modT_ok")
    var_ok, rstd_ok, xn_ok = sem("var_ok"), sem("rstd_ok"), sem("xn_ok")
    h_t, hmod_ok, h_lo = sem("h_t"), sem("hmod_ok"), sem("h_lo")
    split_hi, split_lo, wa_used = sem("split_hi"), sem("split_lo"), sem("wa_used")
    q_ps, q_free, sq_ok, v_ok, ss_ok, rs_ok = sem("q_ps"), sem("q_free"), sem("sq_ok"), sem("v_ok"), sem("ss_ok"), sem("rs_ok")
    qr_ok, qk_t, qk_ok = sem("qr_ok"), sem("qk_t"), sem("qk_ok")
    r_ps, r_ok, pads_ok, xc_ok = sem("r_ps"), sem("r_ok"), sem("pads_ok"), sem("xc_ok")
    bd_zero, bd_in, g_ps, g_ok, th_ok, om_ok, sqr_ok = (sem("bd_zero"), sem("bd_in"), sem("g_ps"), sem("g_ok"), sem("th_ok"),
                                                         sem("om_ok"), sem("sqr_ok"))
    rg_sum, rg_hi, rg_ok, h_done = sem("rg_sum"), sem("rg_hi"), sem("rg_ok"), sem("h_done")
    lam_e, nsp_ok, nb_ok = sem("lam_e"), sem("nsp_ok"), sem("nb_ok")
    brow_in, mod_row = sem("brow_in"), sem("mod_row")
    row_out = [sem("row_out0"), sem("row_out1")]
    s_ps, nmax_ok, exp_ok, prob_ok, pt_ps, pt_ok, pv_ps, cat_hi, cat_lo = (
        sem("s_ps"), sem("nmax_ok"), sem("exp_ok"), sem("prob_ok"), sem("pt_ps"), sem("pt_ok"), sem("pv_ps"),
        sem("cat_hi"), sem("cat_lo"))
    out_ps, out_free, g1_in, var2_ok, rstd2_ok, norm_ok, acc_ok = (
        sem("out_ps"), sem("out_free"), sem("g1_in"), sem("var2_ok"), sem("rstd2_ok"), sem("norm_ok"),
        sem("acc_ok"))
    mod2_in, sc2_in, h_ok, h_out = sem("mod2_in"), sem("sc2_in"), sem("h_ok"), [sem("h_out0"), sem("h_out1")]
    x2_t, h2_ok, lg_ps, lmax_ok, lexp_ok, aff_ok, aff_t = (sem("x2_t"), sem("h2_ok"), sem("lg_ps"), sem("lmax_ok"),
                                                           sem("lexp_ok"), sem("aff_ok"), sem("aff_t"))
    top_ok, top_t, slot_ok = sem("top_ok"), sem("top_t"), sem("slot_ok")
    idx_ready, tok_ready = sem("idx_ready"), sem("tok_ready")
    gathered, x_t = [sem("gathered0"), sem("gathered1")], sem("x_t")
    g2_in, pre_ok, W_hi, W_lo, W_used = sem("g2_in"), sem("pre_ok"), sem("W_hi"), sem("W_lo"), sem("W_used")
    X_hi, X_lo, act_ok, hrow_ok, ht_ps, ht_hi, ht_lo = (
        sem("X_hi"), sem("X_lo"), sem("act_ok"), sem("hrow_ok"), sem("ht_ps"), sem("ht_hi"), sem("ht_lo"))
    y_ok, y_hi, y_lo, cb_ps, cb_free = sem("y_ok"), sem("y_hi"), sem("y_lo"), sem("cb_ps"), sem("cb_free")
    last_ps, gain_ok, y_out_pool = sem("last_ps"), sem("gain_ok"), sem("y_out_pool")
    ln2_in, var3_ok, rstd3_ok, norm3_ok, y_out, pool_out = (
        sem("ln2_in"), sem("var3_ok"), sem("rstd3_ok"), sem("norm3_ok"), sem("y_out"), sem("pool_out"))
    stored = sem("stored")
    dve_seq, pool_seq, hout = sem("dve_seq"), sem("pool_seq"), sem("hout")

    def landed_wait(eng, unit):
        eng.wait_ge(landed[unit % 4], 16 * (unit // 4 + 1))

    U_R, U_MB, U_O, U_G = 8, 12, 24, 28

    block = ctx.enter_context(nc.Block())

    @block.sync
    def _(sp):
        bm_rows = t["b_mod"][0].rearrange("(r p) -> r p", p=P)
        for r0, src in ((R_C, t["c"][0].rearrange("(r p) -> r p", p=P)),
                        (R_CTX, t["c_ctx"].rearrange("(r p) -> r p", p=P)),
                        (R_BM, bm_rows),
                        (R_CW, t["conv_w"][0].rearrange("w (j p) -> (w j) p", p=P)),
                        (R_CB, t["conv_b"][0].rearrange("(j p) -> j p", p=P)),
                        (R_BA, t["b_rg_a"][0].rearrange("d (j p) -> (d j) p", p=P)),
                        (R_BX, t["b_rg_x"][0].rearrange("d (j p) -> (d j) p", p=P)),
                        (R_LAM, t["rg_lambda"][0].rearrange("d (j p) -> (d j) p", p=P)),
                        (R_H0, t["state_h"][0, 0].rearrange("d (j p) -> (d j) p", p=P))):
            sp.dma_start(ring[r0:r0 + src.shape[0], 7, 0:P], src).then_inc(rows_in, 16)
            if r0 == R_C:
                sp.dma_start(consts[:], t["consts"]).then_inc(const_in, 16)

        def stream(u, dst, src):
            v = u - 4
            if u == 3:
                sp.wait_ge(rows_t, 1)
            if v >= U_O:
                sp.wait_ge(split_lo, 16 + 2 * (v - U_O + 1))
            elif v >= U_MB:
                sp.wait_ge(mod_used, 16 + 2 * (v - U_MB + 1))
            elif v >= U_R:
                sp.wait_ge(split_lo, 8 + 2 * (v - U_R + 1))
            elif v >= 0:
                sp.wait_ge(mod_used, 2 * (v + 1))
            sp.dma_start(dst, src).then_inc(landed[u % 4], 16)

        def slots(u, w=1024):
            return ring[:, 2 * (u % 4):2 * (u % 4) + 2, 0:w]

        for u in range(8):
            stream(u, slots(u), w_mod_v[:, 2 * (u % 4):2 * (u % 4) + 2, u // 4, :])
            if u == 7:
                for m in range(4):
                    sp.dma_start(w_qkv[:, 2 * m:2 * m + 2, 0:QKV], w_in_v[:, 2 * m:2 * m + 2, 0:QKV]).then_inc(w_qkv_in[m], 16)
                sp.dma_start(gqk[:, 0, :], t["q_norm_g"][0].partition_broadcast(P)).then_inc(misc_in, 16)
                sp.dma_start(gqk[:, 1, :], t["k_norm_g"][0].partition_broadcast(P)).then_inc(misc_in, 16)
                sp.dma_start(w_rt[:], rt_w).then_inc(misc_in, 16)
        for m in range(4):
            stream(U_R + m, slots(U_R + m), w_in_v[:, 2 * m:2 * m + 2, QKV:QKV + 2 * RG])
        for m in range(12):
            stream(U_MB + m, slots(U_MB + m), w_mod_v[:, 2 * (m % 4):2 * (m % 4) + 2, 2 + m // 4, :])
        for m in range(4):
            stream(U_O + m, slots(U_O + m), w_out_v[:, 2 * m:2 * m + 2, :])
        for m in range(4):
            stream(U_G + m, slots(U_G + m), w_mod_v[:, 2 * m:2 * m + 2, 5, :])

        def expert_dma(unit, e):
            for m in range(2):
                if unit < 8:
                    src = w_gu_v[e][:, 2 * (unit % 4):2 * (unit % 4) + 2, m, unit // 4, :]
                    dst = ring[:, 2 * (unit % 4):2 * (unit % 4) + 2, 512 * m:512 * m + 512]
                else:
                    src = w_dn_v[e][:, 2 * (unit - 8) + m, :]
                    dst = ring[:, 2 * (unit % 4) + m, :]
                sp.dma_start(dst, src).then_inc(landed[unit % 4], 16)

        for m in range(4):
            sp.wait_ge(mod_used, 40 + 2 * (m + 1))
            expert_dma(m, 0)
        with sp.Fori(0, NE // EB - 1) as i:
            for m in range(12 * EB):
                sp.wait_ge(W_lo, i * BODY_PIECES + (2 * m + 2))
                expert_dma((m + 4) % 12, EB * i + (m + 4) // 12)
        for m in range(12 * EB - 4):
            sp.wait_ge(W_lo, (NE // EB - 1) * BODY_PIECES + 2 * m + 2)
            expert_dma((m + 4) % 12, NE - EB + (m + 4) // 12)
        for c in range(CH):
            if c < POOL_LAST:
                sp.wait_ge(y_out_pool, c + 1)
            else:
                sp.wait_ge(y_out, c + 1 - POOL_LAST)
            sp.dma_start(y_s[:, c, :] if c < PC else t["y_prompt"][0], xt[:, c, :]).then_inc(stored, 16)
        sp.wait_ge(stored, 16 * CH)

    @block.gpsimd
    def _(pool):
        seq = [0]

        def link(ins):
            seq[0] += 1
            ins.then_inc(pool_seq, 1)
            pool.wait_ge(pool_seq, seq[0])

        def pow_mhalf(out, in_, n, mul):
            link(pool.tensor_scalar(ptmp[:, 0:n], in_, mul, EPS, ALU.mult, ALU.add))
            return pool.tensor_tensor(out, ptmp[:, 0:n], mhalf[:, 0:n], ALU.pow)

        pool.memset(cT[:], 0.0).then_inc(ct_zero, 1)
        link(pool.memset(mhalf[:], -0.5))
        for h in range(2):
            pool.dma_start(ckd[:].rearrange("p (g h d) -> p g h d", g=2, h=2)[:, :, h, :],
                           t["cache_k"][0, 0]).then_inc(cache_in, 16)
        pool.dma_start(V[:, 4, :], t["cache_v"][0, 0].rearrange("n g d -> n (g d)")).then_inc(cache_in, 16)
        pool.wait_ge(var_ok, 1)
        pow_mhalf(rstd[:], mv[:, :, 1], CH, 1.0).then_inc(rstd_ok, 1)
        for c in range(CH):
            pool.wait_ge(ss_ok, c + 1)
            pow_mhalf(rsq[:, c % 2, :], ssq[:, c % 2, :], 10, 1.0 / HD).then_inc(rs_ok, 1)
        pool.wait_ge(qr_ok, CH)
        pool.wait_ge(v_ok, CH)
        pool.dma_start(t["new_k"][0, 0].rearrange("n g d -> n (g d)"), qr[PC % 2][:, QW:QW + KVW]).then_inc(pool_out, 16)
        pool.dma_start(t["new_v"][0, 0].rearrange("n g d -> n (g d)"), V[:, 5, :]).then_inc(pool_out, 16)
        pool.wait_ge(qk_t, CH)
        pool.memset(BD[0:64, :, 64:128], 0.0).then_inc(bd_zero, 1)
        pool.memset(BD[64:128, :, 0:64], 0.0).then_inc(bd_zero, 1)
        for g, w in ((0, t["w_rg_a"]), (1, t["w_rg_x"])):
            for h in range(2):
                for d in range(2):
                    pool.dma_start(BD[64 * h:64 * h + 64, 8 * g + 4 * d:8 * g + 4 * d + 4, 64 * h:64 * h + 64],
                                   w[0, d, h::2].rearrange("j i o -> i j o")).then_inc(bd_in, 16)
        pool.wait_ge(r_ps, 8)
        link(pool.memset(b_row[:], 0.0))
        for m in range(4):
            if m:
                pool.wait_ge(mod_row, m)
            if m < 3:
                for row in (0, 32):
                    pool.dma_start(b_row[row:row + 1, :], t["b_mod"][:, (m + 2) * D:(m + 3) * D]).then_inc(brow_in, 16)
            if m == 0:
                continue
            for s, row in ((0, 0), (1, 32)):
                pool.dma_start(mods_dram[m - 1, s:s + 1, :], m_row[(m - 1) % 2][row:row + 1, :]).then_inc(row_out[(m - 1) % 2], 16)
        pool.wait_ge(h_done, 2)
        for d, col in ((0, NT - 1), (1, N_S)):
            pool.dma_start(t["new_h"][0, 0, d].rearrange("(j p) -> p j", p=P), hst_out[:, d, :],
                           allow_slow_non_contiguous=True
                           ).then_inc(hout, 16)
        link(pool.tensor_tensor(hst[0][:], hst[0][:], hst[1][:], ALU.add))
        pool.wait_ge(r_ok, 8)
        link(pool.tensor_tensor(hst[0][:], hst[0][:], gel[:], ALU.mult))
        pool.memset(wait_scr[:], 0.0).then_inc(rg_sum, 1)
        for c in range(CH):
            src = x_s[:, c, :] if c < PC else t["x_prompt"][0]
            pool.dma_start(xt[:, c, :], src).then_inc(x_again[c], 16)
        pool.wait_ge(cat_lo, 4)
        pool.wait_ge(cat_hi, 4)
        pool.wait_ge(row_out[0], 64)
        pool.wait_ge(row_out[1], 32)
        for dst, src in ((G1[0], mods_dram[0, 0]), (ln1g, t["ln1_g"][0]), (ln1b, t["ln1_b"][0])):
            pool.dma_start(dst[:], src.partition_broadcast(P)).then_inc(g1_in, 16)
        for dst, src in ((sc2[0], mods_dram[2, 0]), (sh2[0], mods_dram[1, 0]), (G1[1], mods_dram[0, 1]),
                         (sh2[1], mods_dram[1, 1])):
            pool.dma_start(dst[:], src.partition_broadcast(P)).then_inc(mod2_in, 16)

        def rstds(c, done):
            link(pow_mhalf(rstd[:, c:c + 1], mv[:, c, 1:2], 1, 1.0))
            pool.tensor_scalar(nmr[:, c:c + 1], mv[:, c, 0:1], rstd[:, c:c + 1], -1.0, ALU.mult, ALU.mult).then_inc(done, 1)

        def h_store(c):
            pool.wait_ge(h_ok, c + 1)
            pool.dma_start(h2_dram[c * P:(c + 1) * P, :], h2[c % 2][:]).then_inc(h_out[c % 2], 16)

        for c in range(CH):
            pool.wait_ge(var2_ok, 2 * c + 1)
            rstds(c, rstd2_ok)
            if c == PC:
                pool.dma_start(sc2[1][:], mods_dram[2, 1].partition_broadcast(P)).then_inc(sc2_in, 16)
            if c:
                h_store(c - 1)
            pool.wait_ge(var2_ok, 2 * c + 2)
            rstds(c, rstd2_ok)
        h_store(CH - 1)
        pool.wait_ge(h_out[0], 48)
        pool.wait_ge(h_out[1], 32)
        link(pool.memset(b5_row[:], 0.0))
        for row in (0, 32):
            pool.dma_start(b5_row[row:row + 1, :], t["b_mod"][:, 5 * D:6 * D]).then_inc(brow_in, 16)

        def wait_taker():
            pool.tensor_tensor(wait_scr[:], mhalf[:, 0:1], mhalf[:, 0:1], ALU.mult)

        def gather(b, e, count):
            pool.tensor_copy(idx_now[b][:], idx_u[:, e]).then_inc(idx_ready, 1)
            pool.wait_ge(idx_ready, count)
            wait_taker()
            pool.indirect_dma_start(Xg[b][:], None, h2_dram, bass.IndirectOffsetOnAxis(ap=idx_now[b][:], axis=0)
                                    ).then_inc(gathered[b], 16)

        def y_parts(b, count, e1):
            pool.wait_ge(y_ok, count)
            pool.tensor_copy(tok_now[:], idx_slot[:, e1]).then_inc(tok_ready, 1)
            pool.wait_ge(tok_ready, count)
            wait_taker()
            pool.tensor_scalar(ST[b][:], iota_tok[0:SL, :], tok_now[:], None, ALU.is_equal)
            pool.wait_ge(y_hi, count)
            pool.tensor_tensor(Yl[b][:], ysc[:], Yh[b][:].bitcast(F32), ALU.subtract).then_inc(y_lo, 1)

        pool.wait_ge(slot_ok, 1)
        gather(0, slice(0, 1), 1)
        pool.wait_ge(mod_row, 4)
        for s, row in ((0, 0), (1, 32)):
            pool.dma_start(mods_dram[3, s:s + 1, :], m5_row[row:row + 1, :]).then_inc(row_out[1], 16)
        pool.wait_ge(row_out[1], 64)
        pool.dma_start(G2[0:CAP_S, :], mods_dram[3, 0].partition_broadcast(CAP_S)).then_inc(g2_in, 16)
        pool.dma_start(G2[CAP_S:SL, :], mods_dram[3, 1].partition_broadcast(CAP_P)).then_inc(g2_in, 16)
        with pool.Fori(0, NE // EB) as i:
            for b in range(EB):
                if b:
                    pool.wait_ge(x_t, 2 * EB * i + 2 * b)
                    gather((b + 1) % 2, bass.ds(EB * i + (b + 1), 1), EB * i + (b + 2))
                else:
                    pool.wait_ge(x_t, 2 * EB * i + 1)
                    gather(1, bass.ds(EB * i + 1, 1), EB * i + 2)
                y_parts((b - 1) % EB, EB * i + (b + 1), bass.ds(EB * i + b, 1))
        pool.wait_ge(x_t, 2 * NE + 2)
        pool.dma_start(ln2g[:], t["ln2_g"][0].partition_broadcast(P)).then_inc(ln2_in, 16)
        pool.dma_start(ln2b[:], t["ln2_b"][0].partition_broadcast(P)).then_inc(ln2_in, 16)
        for c in range(CH):
            pool.wait_ge(var3_ok, c + 1)
            rstds(c, rstd3_ok)
            if 1 <= c <= POOL_LAST:
                x = xt[:, c - 1, :]
                pool.wait_ge(gain_ok, c)
                pool.wait_ge(ln2_in, 32)
                pool.tensor_tensor(x, x, ln2b[:], ALU.add).then_inc(y_out_pool, 1)
        pool.wait_ge(pool_out, 32)
        pool.wait_ge(hout, 32)

    def pt_evac(act, u):
        h, c = u // CH, u % CH
        act.wait_ge(pt_ps, u + 1)
        if c == 0 and h:
            act.wait_ge(pv_ps, h)
        if c < PC:
            act.activation(PT[:, :, c * P:(c + 1) * P], PS[:, 2048:2048 + NT].rearrange("p (k n) -> p k n", k=5),
                           ACT.Copy).then_inc(pt_ok, 1)
        else:
            act.activation(PTp[:], PS[:, 2048:2048 + P], ACT.Copy).then_inc(pt_ok, 1)

    def cat_evac(act, j):
        act.wait_ge(pv_ps, 2 * j + 2)
        act.activation(Hh[:, j, :], PS[:, 3072:3072 + NT], ACT.Copy).then_inc(cat_hi, 1)

    @block.scalar
    def _(act):
        act.wait_ge(rows_in, 16 * 9)
        for c in range(CH):
            src = x_s[:, c, :] if c < PC else t["x_prompt"][0]
            act.dma_start(xt[:, c, :], src).then_inc(x_in[c], 16)
        act.wait_ge(nb_ok, 1)
        act.wait_ge(ct_zero, 1)
        act.activation(cT[:, :, 0], cols[:, R_C:R_C + 8], ACT.Silu).then_inc(ct_ok, 1)
        act.activation(cT[:, :, 32], cols[:, R_CTX:R_CTX + 8], ACT.Silu).then_inc(ct_ok, 1)
        act.activation(nsp[:, 2, :], lscr[:, 0, :], ACT.Exp, scale=-1.0).then_inc(lam_e, 1)

        def split_w(n, src, w):
            act.activation(WAh[:, n % 8, 0:w], src[:, n % 8, 0:w], ACT.Copy).then_inc(split_hi, 1)

        for g in range(2):
            act.wait_ge(mod_used, KC * (g + 1))
            act.activation(m_rowA[g][:], PS[0:MG, 1024 * g:1024 * g + 1024], ACT.Copy).then_inc(mrow_ok, 1)
            for k in range(4 * g, 4 * g + 4):
                act.wait_ge(w_qkv_in[k // 2], 16)
                split_w(k, w_qkv, QKV)

        act.wait_ge(modT_ok, 2)
        for k in range(KC):
            act.wait_ge(h_t, k + 1)
            if k >= 2:
                act.wait_ge(h_lo, k - 1)
            act.activation(hmod[k % 2][:, 0:N_S], bank(4 + 2 * (k % 2)), ACT.Identity,
                           bias=modT[:, 0, 0, k:k + 1], scale=modT[:, 1, 0, k:k + 1])
            act.activation(hmod[k % 2][:, N_S:NT], bank(5 + 2 * (k % 2), 0, N_P), ACT.Identity,
                           bias=modT[:, 0, 1, k:k + 1], scale=modT[:, 1, 1, k:k + 1]).then_inc(hmod_ok, 1)

        def qk_evac(c):
            act.wait_ge(qk_t, c + 1)
            o = c * P if c < PC else N_S
            act.activation(qT[:, :, o:o + P], bank(4).rearrange("p (j n) -> p j n", j=4), ACT.Copy)
            o = c * P if c < PC else N_S + PAST
            act.activation(kT[:, :, o:o + P], bank(5, 0, 256).rearrange("p (j n) -> p j n", j=2), ACT.Copy).then_inc(qk_ok, 1)

        for c in range(CH):
            if c == CH - 1:
                for n in range(8, 16):
                    landed_wait(act, U_R + (n - 8) // 2)
                    if n < 15:
                        act.wait_ge(wa_used, n - 7)
                    else:
                        act.wait_ge(q_ps, CH)
                    split_w(n, ring, 1024)
            act.wait_ge(q_ps, c + 1)
            b = 2 * (c % 2)
            if c >= 1:
                act.wait_ge(ss_ok, c)
            act.activation(sq[:, 0:QW], bank(b), ACT.Square)
            act.activation(sq[:, QW:QW + KVW], bank(b + 1, 0, KVW), ACT.Square).then_inc(sq_ok, 1)
            act.activation(V[:, c if c < PC else 5, :], bank(b + 1, KVW, 2 * KVW), ACT.Copy).then_inc(v_ok, 1)
            if c >= 2:
                qk_evac(c - 2)
        qk_evac(CH - 2)
        act.wait_ge(pads_ok, 1)
        for j in range(8):
            act.wait_ge(r_ps, j + 1)
            b = 2 * ((j + 1) % 2)
            if j < RJ:
                act.activation(xr[:, j, 2:2 + HN], bank(b, 0, HN), ACT.Copy)
                act.activation(xr[:, j, 2 + HN:2 + N_S], bank(b + 1, 0, N_S - HN), ACT.Copy)
                act.activation(xr[:, j, 518:518 + N_P], bank(b + 1, N_S - HN, HN), ACT.Copy).then_inc(r_ok, 1)
            else:
                act.activation(gel[:, j - RJ, 0:HN], bank(b, 0, HN), ACT.Gelu_apprx_tanh)
                act.activation(gel[:, j - RJ, HN:NT], bank(b + 1, 0, HN), ACT.Gelu_apprx_tanh).then_inc(r_ok, 1)
            if j == 1:
                qk_evac(CH - 1)
                act.wait_ge(qk_t, CH + 1)
                act.activation(kT[:, :, N_S:N_S + PAST], bank(5, 0, 256).rearrange("p (j n) -> p j n", j=2),
                               ACT.Copy).then_inc(qk_ok, 1)
        for d in range(2):
            for n in range(8 * d, 8 * d + 8):
                g, j = (n // 4) % 2, n % 4
                act.wait_ge(g_ps, n + 1)
                b = 2 * ((n + 1) % 2)
                dst = (gate_r if g == 0 else gate_i)[d]
                col = (R_BA if g == 0 else R_BX) + 4 * d + j
                act.activation(dst[:, j, 0:N_S], bank(b), ACT.Sigmoid, bias=cols[:, col:col + 1])
                act.activation(dst[:, j, N_S:NT], bank(b + 1, 0, N_P), ACT.Sigmoid, bias=cols[:, col:col + 1]).then_inc(g_ok, 1)
            act.wait_ge(nsp_ok, 1)
            act.wait_ge(g_ok, 8 * d + 4)
            for j in range(RJ):
                act.activation(thx[d][:, j, :], gate_r[d][:, j, :], ACT.Tanh, scale=nsp[:, 1, 4 * d + j:4 * d + j + 1])
            for j in range(RJ):
                last = act.activation(gate_r[d][:, j, :], gate_r[d][:, j, :], ACT.Exp,
                                      scale=nsp[:, 0, 4 * d + j:4 * d + j + 1])
            last.then_inc(th_ok, 1)
            act.wait_ge(om_ok, d + 1)
            act.activation(thx[d][:], thx[d][:], ACT.Sqrt).then_inc(sqr_ok, 1)

        act.activation(table_scr[:], nsp[:, 0, 0:1], ACT.Exp)
        act.wait_ge(h_done, 2)
        for u in range(NQ * CH):
            h, c = u // CH, u % CH
            w = NT if c < PC else N_P
            act.wait_ge(nmax_ok, u + 1)
            if u >= 3:
                act.wait_ge(pt_ps, u - 2)
            act.activation(prob[u % 3][:, 0:w], PS[:, 1024 * (u % 2):1024 * (u % 2) + w], ACT.Exp,
                           bias=nmax[:, u % 2:u % 2 + 1], scale=SCALE, accum_out=ssum[:, u % 2:u % 2 + 1]).then_inc(exp_ok, 1)
            if u >= 1:
                pt_evac(act, u - 1)
            if c == 2 and h % 2 == 0 and h >= 2:
                cat_evac(act, h // 2 - 1)
            if u in RG_UNITS:
                j = RG_UNITS.index(u)
                act.wait_ge(rg_sum, 1)
                act.activation(Hh[:, 4 + j, :], hst[0][:, j, :], ACT.Copy).then_inc(rg_hi, 1)
            if u in W_UNITS:
                k = W_UNITS.index(u)
                if k == 0:
                    act.wait_ge(rg_ok, RJ)
                landed_wait(act, U_O + k // 2)
                split_w(16 + k, ring, 1024)
        pt_evac(act, NQ * CH - 1)
        cat_evac(act, 3)

        def norm(dst, src, c):
            return act.activation(dst, src, ACT.Identity, bias=nmr[:, c:c + 1], scale=rstd[:, c:c + 1])

        def h2_evac(c):
            act.wait_ge(x2_t, c + 1)
            if c:
                act.wait_ge(lg_ps, c)
            for half in range(2):
                last = act.activation(h2T[:, 4 * half:4 * half + 4, :],
                                      bank(4 + half).rearrange("p (k n) -> p k n", k=4), ACT.Copy)
            last.then_inc(h2_ok, 1)

        for c in range(CH):
            act.wait_ge(rstd2_ok, 2 * c + 1)
            norm(xt[:, c, :], xt[:, c, :], c).then_inc(norm_ok, 1)
            if c:
                h2_evac(c - 1)
            act.wait_ge(rstd2_ok, 2 * c + 2)
            if c >= 2:
                act.wait_ge(x2_t, c - 1)
                act.wait_ge(h_out[c % 2], 16 * (c // 2))
            norm(h2[c % 2][:], xt[:, c, :], c).then_inc(norm_ok, 1)
            act.activation(xt[:, c, :], xt[:, c, :], ACT.Copy, scale=ALPHA).then_inc(acc_ok, 1)
        h2_evac(CH - 1)
        act.wait_ge(lmax_ok, 1)
        act.activation(aff[:], aff[:], ACT.Exp).then_inc(lexp_ok, 1)

        act.wait_ge(lg_ps, CH)
        act.wait_ge(h_out[0], 48)
        act.wait_ge(h_out[1], 32)

        def x_split(b, h, count):
            act.wait_ge(x_t, count)
            act.activation(Xh[b][:, 4 * h:4 * h + 4, :], bank(6, 0, 4 * SL).rearrange("p (k s) -> p k s", k=4),
                           ACT.Copy).then_inc(X_hi, 1)

        def y_split(b, n):
            act.wait_ge(y_ok, n)
            act.activation(Yh[b][:], ysc[:], ACT.Copy).then_inc(y_hi, 1)

        x_split(0, 0, 1)
        x_split(0, 1, 2)
        with act.Fori(0, NE // EB) as i:
            for b in range(EB):
                for q in range(E_PIECES):
                    n = E_PIECES * b + q
                    if q % 2 == 0:
                        act.wait_ge(landed[(q // 2) % 4], 96 * EB * i + (16 * (UNITS_A // 4) + 32 * (3 * b + q // 8 + 1)))
                    act.wait_ge(W_used, BODY_PIECES * i + (n + 1))
                    act.activation(Wh[:, n % WR, :], ring[:, n % RING, :], ACT.Copy).then_inc(W_hi, 1)
                    if q == Y_STEP:
                        y_split((b - 1) % EB, EB * i + (b + 1))
                    if q in X_STEP:
                        h = X_STEP.index(q)
                        x_split((b + 1) % 2, h, 2 * EB * i + (2 * b + h + 3))
                    if q in A_STEP:
                        h = A_STEP.index(q)
                        act.wait_ge(W_used, BODY_PIECES * i + (E_PIECES * b + 8 * h + 8 + WR))
                        act.activation(gate_act[:], bank(2 * h, rows=SL), ACT.Silu).then_inc(act_ok, 1)
                    if q in T_STEP:
                        h = T_STEP.index(q)
                        act.wait_ge(ht_ps, 2 * EB * i + (2 * b + h + 1))
                        act.activation(HTh[:, 4 * h:4 * h + 4, :], bank(6, 0, 4 * SL).rearrange("p (k s) -> p k s", k=4),
                                       ACT.Copy).then_inc(ht_hi, 1)
        y_split(EB - 1, NE + 1)
        for c in range(CH):
            act.wait_ge(rstd3_ok, c + 1)
            b = 1024 * (c % 4)
            norm(xt[:, c, :], PS[:, b:b + 1024], c).then_inc(norm3_ok, 1)

    @block.tensor
    def _(pe):
        def three(out, w, x, first, last):
            pe.matmul(out, w[0], x[0], start=first, stop=False)
            pe.matmul(out, w[1], x[0], start=False, stop=False)
            return pe.matmul(out, w[0], x[1], start=False, stop=last)

        pe.wait_ge(rows_in, 16 * 9)
        pe.wait_ge(const_in, 16)
        pe.transpose(bank(7, 0, R_END), ring[0:R_END, 7, 0:P], ident[0:R_END, 0:R_END]).then_inc(rows_t, 1)

        def mod_group(g, u0):
            b = [0, 2, 4, 6, 4, 0][g]
            for k in range(KC):
                if k % 2 == 0:
                    landed_wait(pe, u0 + k // 2)
                for half in range(2):
                    last = pe.matmul(bank(b + half, rows=MG), cT[:, k, :],
                                     ring[:, k, 512 * half:512 * half + 512], start=(k == 0), stop=(k == KC - 1))
                last.then_inc(mod_used, 1)

        def row_transposes(src, b):
            for k in range(KC):
                last = pe.transpose(bank(b, MG * k, MG * k + MG), src[:, k * P:(k + 1) * P], ident[0:MG, 0:MG])
            last.then_inc(mrow_t, 1)

        pe.wait_ge(ct_ok, 2)
        mod_group(0, 0)
        mod_group(1, 4)
        for g in range(2):
            pe.wait_ge(mrow_ok, g + 1)
            row_transposes(m_rowA[g], 4 + g)
        pe.wait_ge(xn_ok, CH)
        pe.wait_ge(modT_ok, 2)
        for k in range(KC):
            if k >= 2:
                pe.wait_ge(hmod_ok, k - 1)
            for c in range(CH):
                b = (4 if c < PC else 5) + 2 * (k % 2)
                o = c * P if c < PC else 0
                last = pe.transpose(bank(b, o, o + P), xt[:, c, k * P:(k + 1) * P], ident)
            last.then_inc(h_t, 1)

        def qk_transposes(c):
            pe.wait_ge(qr_ok, c + 1)
            if c:
                pe.wait_ge(qk_ok, c)
            else:
                pe.wait_ge(hmod_ok, KC)
            for j in range(4):
                pe.transpose(bank(4, j * P, (j + 1) * P), qr[c % 2][:, j * P:(j + 1) * P], ident)
            for j in range(2):
                last = pe.transpose(bank(5, j * P, (j + 1) * P), kd[c % 2][:, j * P:(j + 1) * P], ident)
            last.then_inc(qk_t, 1)

        pe.wait_ge(mrow_ok, 2)
        for c in range(CH):
            b = 2 * (c % 2)
            if c >= 2:
                pe.wait_ge(q_free, c - 1)
                pe.wait_ge(v_ok, c - 1)
            for k in range(KC):
                if c == 0:
                    pe.wait_ge(h_lo, k + 1)
                    pe.wait_ge(split_lo, k + 1)
                x = (Hh[:, k, c * P:(c + 1) * P], Hl[:, k, c * P:(c + 1) * P])
                three(bank(b), x, (WAh[:, k, 0:QW], WAl[:, k, 0:QW]), k == 0, k == KC - 1)
                last = three(bank(b + 1, 0, 2 * KVW), x, (WAh[:, k, QW:QKV], WAl[:, k, QW:QKV]), k == 0, k == KC - 1)
                if c == CH - 1 and k < KC - 1:
                    last.then_inc(wa_used, 1)
            last.then_inc(q_ps, 1)
            if c >= 2:
                qk_transposes(c - 2)
        for j in range(8):
            b = 2 * ((j + 1) % 2)
            if j < 2:
                pe.wait_ge(q_free, CH - 1 + j)
                pe.wait_ge(v_ok, CH - 1 + j)
            else:
                pe.wait_ge(r_ok, j - 1)
            for k in range(KC):
                if j == 0:
                    pe.wait_ge(split_lo, 8 + k + 1)
                w = (WAh[:, k, j * P:(j + 1) * P], WAl[:, k, j * P:(j + 1) * P])
                three(bank(b, 0, HN), w, (Hh[:, k, 0:HN], Hl[:, k, 0:HN]), k == 0, k == KC - 1)
                last = three(bank(b + 1, 0, HN), w, (Hh[:, k, HN:NT], Hl[:, k, HN:NT]), k == 0, k == KC - 1)
            last.then_inc(r_ps, 1)
            if j == 0:
                qk_transposes(CH - 2)
            if j == 1:
                qk_transposes(CH - 1)
                pe.wait_ge(qk_ok, CH)
                pe.wait_ge(cache_in, 48)
                for m in range(2):
                    last = pe.transpose(bank(5, m * P, (m + 1) * P), ckd[:, m * P:(m + 1) * P], ident)
                last.then_inc(qk_t, 1)
        pe.wait_ge(bd_zero, 2)
        pe.wait_ge(bd_in, 16 * 8)
        for n in range(16):
            d, g, j = n // 8, (n // 4) % 2, n % 4
            b = 2 * ((n + 1) % 2)
            if n < 2:
                pe.wait_ge(r_ok, 7 + n)
            else:
                pe.wait_ge(g_ok, n - 1)
            if n < 4:
                pe.wait_ge(xc_ok, j + 1)
            if n == 8:
                pe.wait_ge(qk_ok, CH + 1)
                mod_group(2, U_MB)
            w = BD[:, 8 * g + 4 * d + j, :]
            pe.matmul(bank(b), w, XC[:, j, 0:N_S], start=True, stop=True)
            pe.matmul(bank(b + 1, 0, N_P), w, XC[:, j, N_S:NT], start=True, stop=True).then_inc(g_ps, 1)
        mod_group(3, U_MB + 4)
        def scores(u):
            h, c = u // CH, u % CH
            rows = slice(64 * (h % 2), 64 * (h % 2) + 64)
            j, g, b = h // 2, h // (NQ // NKV), 2 * (u % 2)
            if u >= 2:
                pe.wait_ge(exp_ok, u - 1)
            if c < PC:
                q = qT[rows, j, c * P:(c + 1) * P]
                pe.matmul(bank(b), q, kT[rows, g, 0:N_S], start=True, stop=True)
                pe.matmul(bank(b + 1, 0, PAST), q, kT[rows, g, N_S:N_S + PAST], start=True, stop=True).then_inc(s_ps, 1)
            else:
                pe.matmul(bank(b, 0, N_P), qT[rows, j, N_S:NT], kT[rows, g, N_S + PAST:N_S + PAST + N_P],
                          start=True, stop=True).then_inc(s_ps, 1)

        def values(h):
            pe.wait_ge(pt_ok, (h + 1) * CH)
            if h == 0:
                pe.wait_ge(mod_row, 2)
            elif h % 2 == 0:
                pe.wait_ge(cat_lo, h // 2)
            g, r0 = h // (NQ // NKV), 64 * (h % 2)
            for k in range(5):
                pe.matmul(PS[r0:r0 + 64, 3072:3584], V[:, k, g * HD:(g + 1) * HD], PT[:, k, :],
                          start=(k == 0), stop=(k == 4))
            pe.matmul(PS[r0:r0 + 64, 3584:3584 + N_P], V[:, 5, g * HD:(g + 1) * HD], PTp[:],
                      start=True, stop=True).then_inc(pv_ps, 1)

        pe.wait_ge(g_ok, 16)
        scores(0)
        scores(1)
        pe.wait_ge(mod_row, 1)
        mod_group(4, U_MB + 8)
        for u in range(NQ * CH):
            h, c = u // CH, u % CH
            if u + 2 < NQ * CH:
                scores(u + 2)
            if c == 0 and h:
                values(h - 1)
            pe.wait_ge(prob_ok, u + 1)
            if u:
                pe.wait_ge(pt_ok, u)
            else:
                pe.wait_ge(mod_row, 3)
            for k in range(5 if c < PC else 1):
                last = pe.transpose(PS[:, 2048 + k * P:2048 + (k + 1) * P], prob[u % 3][:, k * P:(k + 1) * P], ident)
            last.then_inc(pt_ps, 1)
        values(NQ - 1)

        def x2_transposes(c):
            pe.wait_ge(h_ok, c + 1)
            if c:
                pe.wait_ge(h2_ok, c)
            for k in range(KC):
                last = pe.transpose(PS[:, 2048 + k * P:2048 + (k + 1) * P], h2[c % 2][:, k * P:(k + 1) * P], ident)
            last.then_inc(x2_t, 1)

        def logits(c):
            pe.wait_ge(h2_ok, c + 1)
            for k in range(KC):
                last = pe.matmul(bank(6, c * NE, (c + 1) * NE), h2T[:, k, :], w_rt[:, k, :], start=(k == 0), stop=(k == KC - 1))
            last.then_inc(lg_ps, 1)

        pe.wait_ge(cat_lo, 4)
        pe.wait_ge(rg_ok, RJ)
        pe.wait_ge(misc_in, 48)
        for c in range(CH):
            b = 2 * (c % 2)
            if c >= 2:
                pe.wait_ge(out_free, c - 1)
            for k in range(KC):
                if c == 0:
                    pe.wait_ge(split_lo, 16 + k + 1)
                x = (Hh[:, k, c * P:(c + 1) * P], Hl[:, k, c * P:(c + 1) * P])
                three(bank(b), x, (WAh[:, k, 0:512], WAl[:, k, 0:512]), k == 0, k == KC - 1)
                last = three(bank(b + 1), x, (WAh[:, k, 512:1024], WAl[:, k, 512:1024]), k == 0, k == KC - 1)
            last.then_inc(out_ps, 1)
            if c >= 2:
                x2_transposes(c - 2)
            if c >= 3:
                logits(c - 3)
        logits(CH - 3)
        for c in (CH - 2, CH - 1):
            x2_transposes(c)
            logits(c)
        pe.wait_ge(aff_ok, 1)
        for c in range(CH):
            out = PS[0:NE, 3584 + c * P:3584 + (c + 1) * P] if c < PC else PS[0:NE, 3072 + 256:3072 + 384]
            last = pe.transpose(out, aff[:, c, :], ident)
        last.then_inc(aff_t, 1)
        pe.wait_ge(out_free, CH)
        mod_group(5, U_G)
        pe.wait_ge(top_ok, 1)
        pe.transpose(bank(7, 0, NE, rows=SL), topf[:], ident[0:NE, 0:NE])
        pe.transpose(bank(7, 16, 16 + NE, rows=SL), topv[:], ident[0:NE, 0:NE]).then_inc(top_t, 1)

        def x_transposes(b, h, count):
            if h == 0:
                pe.wait_ge(gathered[b], count)
            for m in range(4):
                last = pe.transpose(bank(6, m * SL, (m + 1) * SL), Xg[b][:, (4 * h + m) * P:(4 * h + m + 1) * P],
                                    ident[0:SL, 0:SL])
            last.then_inc(x_t, 1)

        x_transposes(0, 0, 16)
        pe.wait_ge(X_lo, 1)
        x_transposes(0, 1, 16)
        pe.wait_ge(pre_ok, 1)
        for half in range(2):
            last = pe.matmul(bank(4 + half, rows=SL), ST[2][:, 0:SL], ST[2][:, 0:512], start=True, stop=True)
        last.then_inc(W_used, WR)

        def combine(out, n, pair):
            c, half = n // 2, n % 2
            for b in pair:
                lhs = ST[b][:, c * P:(c + 1) * P]
                pe.matmul(out, lhs, Yh[b][:, 512 * half:512 * half + 512], start=(b == pair[0]), stop=False)
                last = pe.matmul(out, lhs, Yl[b][:, 512 * half:512 * half + 512], start=False, stop=(b == pair[1]))
            return last

        with pe.Fori(0, NE // EB) as i:
            for b in range(EB):
                for q in range(E_PIECES):
                    n = E_PIECES * b + q
                    s = n % WR
                    if q == 0:
                        pe.wait_ge(X_lo, 2 * EB * i + (2 * b + 2))
                    if q in (0, 8):
                        pe.wait_ge(hrow_ok, 2 * EB * i + (2 * b + q // 8 + 1))
                    if q == 16:
                        pe.wait_ge(y_ok, EB * i + (b + 1))
                    if q in (16, 20):
                        pe.wait_ge(ht_lo, 2 * EB * i + (2 * b + (q - 16) // 4 + 1))
                    pe.wait_ge(W_lo, BODY_PIECES * i + (n + 1))
                    k = q % 8
                    if q < 16:
                        x, o0 = (Xh[b % 2][:, k, :], Xl[b % 2][:, k, :]), 2 * (q // 8)
                    else:
                        x, o0 = (HTh[:, k, :], HTl[:, k, :]), 4
                    for half in range(2):
                        cs = slice(512 * half, 512 * half + 512)
                        last = three(bank(o0 + half, rows=SL), x, (Wh[:, s, cs], Wl[:, s, cs]), k == 0, k == 7)
                    last.then_inc(W_used, 1)
                    if q in PX_STEP:
                        h = PX_STEP.index(q)
                        if h == 1:
                            pe.wait_ge(X_lo, 2 * EB * i + (2 * b + 3))
                        x_transposes((b + 1) % 2, h, 16 * (EB // 2) * i + 16 * ((b + 1) // 2 + 1))
                    if q in PT_STEP:
                        h = PT_STEP.index(q)
                        pe.wait_ge(hrow_ok, 2 * EB * i + (2 * b + h + 3))
                        if h == 0:
                            pe.wait_ge(X_lo, 2 * EB * i + (2 * b + 4))
                        else:
                            pe.wait_ge(ht_lo, 2 * EB * i + (2 * b + 1))
                        for m in range(4):
                            last = pe.transpose(bank(6, m * SL, (m + 1) * SL), hrow[:, m * P:(m + 1) * P],
                                                ident[0:SL, 0:SL])
                        last.then_inc(ht_ps, 1)
                    p, r = n // 48, n % 48 - CB_START
                    if r >= 0 and r % CB_EVERY == 0 and r // CB_EVERY < 10:
                        g = r // CB_EVERY
                        if g == 0:
                            pe.wait_ge(y_lo, EB * i + (2 * p + 2))
                        pe.wait_ge(cb_free, 20 * i + (10 * p + g + 1))
                        combine(bank(7), g, (2, 3) if p == 0 else (0, 1)).then_inc(cb_ps, 1)
        def residual_last(n):
            c, half = n // 2, n % 2
            pe.matmul(bank(n % 8), ident, xt[:, c, 512 * half:512 * half + 512], start=True, stop=False)

        def combine_one(n, b):
            c, half = n // 2, n % 2
            lhs = ST[b][:, c * P:(c + 1) * P]
            pe.matmul(bank(n % 8), lhs, Yh[b][:, 512 * half:512 * half + 512], start=False, stop=False)
            return pe.matmul(bank(n % 8), lhs, Yl[b][:, 512 * half:512 * half + 512], start=False, stop=(b == 3))

        pe.wait_ge(hrow_ok, 2 * NE + 2)
        pe.wait_ge(cb_free, 20 * (NE // EB) + 1)
        pe.wait_ge(y_lo, NE + 1)
        for n in range(4):
            residual_last(n)
            combine_one(n, 2)
        pe.wait_ge(y_lo, NE + 2)
        pe.wait_ge(X_lo, 2 * NE + 2)
        for n in range(2 * CH):
            if n == 8:
                pe.wait_ge(var3_ok, 1)
                pe.wait_ge(norm3_ok, 1)
            if n >= 4:
                residual_last(n)
                combine_one(n, 2)
            last = combine_one(n, 3)
            if n % 2:
                last.then_inc(last_ps, 1)

    @block.vector
    def _(dve):
        seq = [0]

        def link(ins):
            seq[0] += 1
            ins.then_inc(dve_seq, 1)
            dve.wait_ge(dve_seq, seq[0])

        def layer_stats(src, c):
            for h in range(2):
                last = dve.bn_stats(stats[:, c, h, :], src[:, 512 * h:512 * h + 512])
            link(last)
            return dve.bn_aggr(mv[:, c, :], stats[:, c])

        dve.wait_ge(rows_t, 1)
        link(dve.tensor_copy(cols[:], bank(7, 0, R_END)))
        link(dve.tensor_scalar(lscr[:, 1, :], cols[:, R_LAM:R_LAM + 8], -1.0, None, ALU.mult))
        dve.tensor_tensor(lscr[:, 0, :], lscr[:, 1, :], cols[:, R_LAM:R_LAM + 8], ALU.max).then_inc(nb_ok, 1)
        for c in range(CH):
            dve.wait_ge(x_in[c], 16)
            last = layer_stats(xt[:, c, :], c)
        last.then_inc(var_ok, 1)
        dve.wait_ge(lam_e, 1)
        u, s, z, acc = nsp[:, 2, :], lscr[:, 2, :], lscr[:, 3, :], nsp[:, 1, :]
        link(dve.tensor_scalar(s, u, 2.0, None, ALU.add))
        link(dve.reciprocal(z, s))
        link(dve.tensor_tensor(s, u, z, ALU.mult))
        link(dve.tensor_tensor(z, s, s, ALU.mult))
        link(dve.tensor_scalar(acc, z, 1.0 / 19.0, None, ALU.mult))
        for m in (17, 15, 13, 11, 9, 7, 5, 3):
            link(dve.scalar_tensor_tensor(acc, acc, 1.0 / m, z, ALU.add, ALU.mult))
        link(dve.scalar_tensor_tensor(acc, acc, 1.0, s, ALU.add, ALU.mult))
        link(dve.tensor_scalar(z, lscr[:, 1, :], 0.0, C_LRU, ALU.max, ALU.mult))
        link(dve.scalar_tensor_tensor(acc, acc, 2.0 * C_LRU, z, ALU.mult, ALU.add))
        dve.tensor_scalar(nsp[:, 0, :], acc, -1.0, None, ALU.mult).then_inc(nsp_ok, 1)

        dve.wait_ge(rstd_ok, 1)
        for c in range(CH):
            dve.tensor_scalar(xt[:, c, :], xt[:, c, :], mv[:, c, 0:1], rstd[:, c:c + 1],
                              ALU.subtract, ALU.mult).then_inc(xn_ok, 1)

        def mod_cols(g, b, w, plus):
            dve.wait_ge(mrow_t, g + 1)
            src = bank(b, 0, MG * KC).rearrange("p (k m) -> p k m", m=MG)
            for s_ in range(2):
                last = dve.scalar_tensor_tensor(modT[:, w, s_, :], src[:, :, 32 * s_], plus,
                                                cols[:, R_BM + 8 * g:R_BM + 8 * g + 8], ALU.add, ALU.add)
            last.then_inc(modT_ok, 1)

        def split_lo_w(n, src, w):
            dve.wait_ge(split_hi, n + 1)
            dve.tensor_tensor(WAl[:, n % 8, 0:w], src[:, n % 8, 0:w], WAh[:, n % 8, 0:w].bitcast(F32),
                              ALU.subtract).then_inc(split_lo, 1)

        for k in range(4):
            split_lo_w(k, w_qkv, QKV)
        mod_cols(0, 4, 0, 0.0)
        mod_cols(1, 5, 1, 1.0)
        for k in range(4, KC):
            split_lo_w(k, w_qkv, QKV)
        for k in range(KC):
            dve.wait_ge(hmod_ok, k + 1)
            link(dve.tensor_copy(Hh[:, k, :], hmod[k % 2][:]))
            dve.tensor_tensor(Hl[:, k, :], hmod[k % 2][:], Hh[:, k, :].bitcast(F32), ALU.subtract).then_inc(h_lo, 1)

        dve.wait_ge(h_t, KC)
        dve.memset(xr[:, :, 0:2], 0.0)
        dve.memset(xr[:, :, 514:518], 0.0)
        dve.memset(xr[:, :, 646:648], 0.0).then_inc(pads_ok, 1)

        def heads(ap, n):
            return ap.rearrange("p (h d) -> p h d", h=n)

        def pairs(ap):
            return ap.rearrange("p (h a b n) -> p h a b n", h=10, a=2, b=2)

        for c in range(CH):
            b = 2 * (c % 2)
            dve.wait_ge(sq_ok, c + 1)
            dve.tensor_reduce(ssq[:, c % 2, :], heads(sq[:], 10), AX.X, ALU.add).then_inc(ss_ok, 1)
            if c == 0:
                dve.wait_ge(misc_in, 48)
            dve.wait_ge(rs_ok, c + 1)
            dve.wait_ge(v_ok, c + 1)
            dve.tensor_tensor(heads(qn[:, 0:QW], 8), heads(bank(b), 8),
                              rsq[:, c % 2, 0:8].unsqueeze(2).broadcast_to([P, 8, HD]), ALU.mult)
            last = dve.tensor_tensor(heads(qn[:, QW:640], 2), heads(bank(b + 1, 0, KVW), 2),
                                     rsq[:, c % 2, 8:10].unsqueeze(2).broadcast_to([P, 2, HD]), ALU.mult)
            last.then_inc(q_free, 1)
            dve.wait_ge(q_free, c + 1)
            dst = qn if c < PC else qr[c % 2]
            if c >= 2:
                dve.wait_ge(qk_t, c - 1)
            dve.tensor_tensor(heads(dst[:, 0:QW], 8), heads(qn[:, 0:QW], 8),
                              gqk[:, 0, :].unsqueeze(1).broadcast_to([P, 8, HD]), ALU.mult)
            link(dve.tensor_tensor(heads(dst[:, QW:640], 2), heads(qn[:, QW:640], 2),
                                   gqk[:, 1, :].unsqueeze(1).broadcast_to([P, 2, HD]), ALU.mult))
            if c < PC:
                def cs(w):
                    return rope[:, c, w, :].rearrange("p (a n) -> p a n", a=2).unsqueeze(1).broadcast_to([P, 10, 2, 16])
                x1, x2 = pairs(qn[:])[:, :, :, 0, :], pairs(qn[:])[:, :, :, 1, :]
                y1, y2 = pairs(qr[c % 2][:])[:, :, :, 0, :], pairs(qr[c % 2][:])[:, :, :, 1, :]
                t1 = rt[:, 0, :].rearrange("p (h a n) -> p h a n", h=10, a=2)
                t2 = rt[:, 1, :].rearrange("p (h a n) -> p h a n", h=10, a=2)
                dve.tensor_tensor(t1, x1, cs(0), ALU.mult)
                link(dve.tensor_tensor(t2, x2, cs(1), ALU.mult))
                link(dve.tensor_tensor(y1, t1, t2, ALU.subtract))
                dve.tensor_tensor(t1, x1, cs(1), ALU.mult)
                link(dve.tensor_tensor(t2, x2, cs(0), ALU.mult))
                link(dve.tensor_tensor(y2, t1, t2, ALU.add))
            dve.tensor_copy(kd[c % 2][:].rearrange("p (g h d) -> p g h d", g=2, h=2),
                            heads(qr[c % 2][:, QW:640], 2).unsqueeze(2).broadcast_to([P, 2, 2, HD])).then_inc(qr_ok, 1)
            if c == CH - 2:
                for n in range(8, 16):
                    split_lo_w(n, ring, 1024)

        dve.wait_ge(qk_t, CH + 1)
        dve.wait_ge(pool_out, 32)
        for j in range(RJ):
            dve.wait_ge(r_ok, j + 1)
            for o0, i0, w in ((0, 0, N_S), (N_S, 516, N_P)):
                def tap(m):
                    return xr[:, j, i0 + m:i0 + m + w]
                cw = [cols[:, R_CW + 4 * m + j:R_CW + 4 * m + j + 1] for m in range(4)]
                out = XC[:, j, o0:o0 + w]
                link(dve.tensor_scalar(out, tap(0), cw[0], cols[:, R_CB + j:R_CB + j + 1], ALU.mult, ALU.add))
                for m in (1, 2):
                    link(dve.scalar_tensor_tensor(out, tap(m), cw[m], out, ALU.mult, ALU.add))
                last = dve.scalar_tensor_tensor(out, tap(3), cw[3], out, ALU.mult, ALU.add)
            last.then_inc(xc_ok, 1)

        def mod_row_sum(m):
            dve.wait_ge(mod_used, KC * (m + 3))
            dve.wait_ge(brow_in, 32 * (m + 1))
            if m == 2:
                dve.wait_ge(row_out[0], 32)
            out, bias, b = [(m_row[0], b_row, 2048), (m_row[1], b_row, 3072), (m_row[0], b_row, 2048), (m5_row, b5_row, 0)][m]
            dve.scalar_tensor_tensor(out[:], PS[0:MG, b:b + 1024], 1.0 if m == 2 else 0.0, bias[:],
                                     ALU.add, ALU.add).then_inc(mod_row, 1)

        dve.wait_ge(xc_ok, RJ)
        for d in range(2):
            dve.wait_ge(g_ok, 8 * (d + 1))
            link(dve.tensor_tensor(gate_i[d][:], gate_i[d][:], XC[:], ALU.mult))
            dve.wait_ge(th_ok, d + 1)
            link(dve.tensor_tensor(hst[d][:], gate_r[d][:], gate_r[d][:], ALU.mult))
            dve.scalar_tensor_tensor(thx[d][:].rearrange("p j n -> p (j n)"), hst[d][:].rearrange("p j n -> p (j n)"), 1.0,
                                     thx[d][:].rearrange("p j n -> p (j n)"), ALU.add, ALU.mult).then_inc(om_ok, 1)
            dve.wait_ge(sqr_ok, d + 1)
            link(dve.tensor_tensor(gate_i[d][:], thx[d][:], gate_i[d][:], ALU.mult))
            for j in range(RJ):
                h0 = cols[:, R_H0 + 4 * d + j:R_H0 + 4 * d + j + 1]
                for o0, w, init in ((0, N_S, h0), (N_S, N_P, 0.0)):
                    a_, b_, h_ = (x_[:, j, o0:o0 + w] for x_ in (gate_r[d], gate_i[d], hst[d]))
                    if d:
                        a_, b_, h_ = a_[:, ::-1], b_[:, ::-1], h_[:, ::-1]
                    last = dve.tensor_tensor_scan(h_, a_, b_, init, ALU.mult, ALU.add)
            link(last)
            col = NT - 1 if d == 0 else N_S
            dve.tensor_copy(hst_out[:, d, :], hst[d][:, :, col]).then_inc(h_done, 1)
            mod_row_sum(d)

        def cat_lo_evac(j):
            dve.wait_ge(cat_hi, j + 1)
            dve.tensor_tensor(Hl[:, j, :], PS[:, 3072:3072 + NT], Hh[:, j, :].bitcast(F32), ALU.subtract).then_inc(cat_lo, 1)

        for u in range(NQ * CH + 1):
            h, c = u // CH, u % CH
            if u < NQ * CH:
                w = NT if c < PC else N_P
                dve.wait_ge(s_ps, u + 1)
                if u >= 2:
                    dve.wait_ge(exp_ok, u - 1)
                link(dve.tensor_reduce(smax[:, u % 2:u % 2 + 1], PS[:, 1024 * (u % 2):1024 * (u % 2) + w], AX.X, ALU.max))
                dve.tensor_scalar(nmax[:, u % 2:u % 2 + 1], smax[:, u % 2:u % 2 + 1], -SCALE, None, ALU.mult).then_inc(nmax_ok, 1)
            if u:
                v = u - 1
                w = NT if v % CH < PC else N_P
                dve.wait_ge(exp_ok, u)
                link(dve.reciprocal(rsum[:, v % 2:v % 2 + 1], ssum[:, v % 2:v % 2 + 1]))
                dve.tensor_scalar(prob[v % 3][:, 0:w], prob[v % 3][:, 0:w], rsum[:, v % 2:v % 2 + 1], None,
                                  ALU.mult).then_inc(prob_ok, 1)
            if u < NQ * CH and c == 3 and h % 2 == 0 and h >= 2:
                cat_lo_evac(h // 2 - 1)
            if u == 1:
                mod_row_sum(2)
            if u - 1 in RG_UNITS:
                j = RG_UNITS.index(u - 1)
                dve.wait_ge(rg_hi, j + 1)
                dve.tensor_tensor(Hl[:, 4 + j, :], hst[0][:, j, :], Hh[:, 4 + j, :].bitcast(F32), ALU.subtract).then_inc(rg_ok, 1)
            if u - 1 in W_UNITS:
                dve.wait_ge(row_out[0], 64)
                dve.wait_ge(row_out[1], 32)
                split_lo_w(16 + W_UNITS.index(u - 1), ring, 1024)
        cat_lo_evac(3)

        def residual(c):
            x = xt[:, c, :]
            dve.wait_ge(out_ps, c + 1)
            if c >= 2:
                dve.wait_ge(x2_t, c - 1)
                dve.wait_ge(h_out[c % 2], 16 * (c // 2))
            dve.tensor_tensor(h2[c % 2][:], PS[:, 1024 * (c % 2):1024 * (c % 2) + 1024], G1[0 if c < PC else 1][:],
                              ALU.mult).then_inc(out_free, 1)
            dve.wait_ge(x_again[c], 16)
            dve.wait_ge(out_free, c + 1)
            link(dve.scalar_tensor_tensor(x, x, ALPHA, h2[c % 2][:], ALU.mult, ALU.add))
            layer_stats(x, c).then_inc(var2_ok, 1)

        def post_norm(c):
            x = xt[:, c, :]
            dve.wait_ge(norm_ok, 2 * c + 1)
            link(dve.tensor_tensor(x, x, ln1g[:], ALU.mult))
            link(dve.tensor_tensor(x, x, ln1b[:], ALU.add))
            layer_stats(x, c).then_inc(var2_ok, 1)

        def modulated(c):
            s_ = 0 if c < PC else 1
            dve.wait_ge(norm_ok, 2 * c + 2)
            if c == 0:
                dve.wait_ge(mod2_in, 64)
            if c == PC:
                dve.wait_ge(sc2_in, 16)
            link(dve.tensor_tensor(h2[c % 2][:], h2[c % 2][:], sc2[s_][:], ALU.mult))
            dve.tensor_tensor(h2[c % 2][:], h2[c % 2][:], sh2[s_][:], ALU.add).then_inc(h_ok, 1)

        dve.wait_ge(g1_in, 48)
        for c in range(CH + 1):
            if c < CH:
                residual(c)
            if c:
                modulated(c - 1)
            if c < CH:
                post_norm(c)
        dve.wait_ge(lg_ps, CH)
        lg = bank(6, 0, CH * NE).rearrange("p (c e) -> p c e", c=CH)
        link(dve.tensor_reduce(rmax[:], lg, AX.X, ALU.max))
        dve.tensor_tensor(aff[:], lg, rmax[:].unsqueeze(2).broadcast_to([P, CH, NE]), ALU.subtract).then_inc(lmax_ok, 1)
        dve.wait_ge(lexp_ok, 1)
        link(dve.tensor_reduce(rmax[:], aff[:], AX.X, ALU.add))
        link(dve.reciprocal(rmax[:], rmax[:]))
        dve.tensor_tensor(aff[:], aff[:], rmax[:].unsqueeze(2).broadcast_to([P, CH, NE]), ALU.mult).then_inc(aff_ok, 1)
        dve.wait_ge(aff_t, 1)
        dve.wait_ge(out_ps, CH)
        dve.tensor_copy(affw[:, 0:N_S], PS[0:NE, 3584:4096])
        link(dve.tensor_copy(affw[:, N_S:NT], PS[0:NE, 3072 + 256:3072 + 384]))
        for a0, w, v0, cap in ((0, N_S, 0, CAP_S), (N_S, N_P, CAP_S, CAP_P)):
            vals = affw[:, a0:a0 + w]
            if a0:
                mod_row_sum(3)
            for r in range(cap // 8):
                tv = topv[:, v0 + 8 * r:v0 + 8 * r + 8]
                link(dve.max(tv, vals))
                link(dve.max_index(topi[:, v0 + 8 * r:v0 + 8 * r + 8], tv, vals))
                link(dve.match_replace(vals, tv, vals, -1.0))
        dve.tensor_copy(topf[:, 0:CAP_S], topi[:, 0:CAP_S])
        dve.tensor_scalar(topf[:, CAP_S:SL], topi[:, CAP_S:SL], float(N_S), None, ALU.add).then_inc(top_ok, 1)
        dve.wait_ge(top_t, 1)
        dve.memset(idx_slot[:, 0:1], -1.0)
        dve.memset(g_slot[:, 0:1], 0.0)
        dve.tensor_copy(idx_u[:, 0:NE], bank(7, 0, NE, rows=SL))
        dve.tensor_copy(idx_u[:, NE:NE + 1], bank(7, 0, 1, rows=SL))
        dve.tensor_copy(idx_slot[:, 1:NE + 1], bank(7, 0, NE, rows=SL))
        dve.tensor_copy(g_slot[:, 1:NE + 1], bank(7, 16, 16 + NE, rows=SL)).then_inc(slot_ok, 1)

        dve.memset(Yh[2][:].bitcast(F32), 0.0).then_inc(cb_free, 1)
        dve.memset(Yl[2][:].bitcast(F32), 0.0).then_inc(y_lo, 1)
        dve.memset(ST[2][:].bitcast(F32), 0.0).then_inc(pre_ok, 1)

        def x_lo(b, h, count):
            dve.wait_ge(X_hi, count)
            dve.tensor_tensor(Xl[b][:, 4 * h:4 * h + 4, :], bank(6, 0, 4 * SL).rearrange("p (k s) -> p k s", k=4),
                              Xh[b][:, 4 * h:4 * h + 4, :].bitcast(F32), ALU.subtract).then_inc(X_lo, 1)

        def y_evac(count, e1, used):
            dve.wait_ge(W_used, used)
            dve.wait_ge(g2_in, 32)
            dve.wait_ge(y_lo, count)
            dve.scalar_tensor_tensor(ysc[:], PS[0:SL, 2048:3072], g_slot[:, e1], G2[:], ALU.mult, ALU.mult).then_inc(y_ok, 1)

        x_lo(0, 0, 1)
        x_lo(0, 1, 2)
        dve.wait_ge(pre_ok, 1)
        dve.tensor_copy(hrow[:, 0:1], g_slot[:, 0:1]).then_inc(hrow_ok, 2)
        dve.wait_ge(acc_ok, CH)
        with dve.Fori(0, NE // EB) as i:
            for b in range(EB):
                for q in range(E_PIECES):
                    n = E_PIECES * b + q
                    dve.wait_ge(W_hi, BODY_PIECES * i + (n + 1))
                    dve.tensor_tensor(Wl[:, n % WR, :], ring[:, n % RING, :], Wh[:, n % WR, :].bitcast(F32),
                                      ALU.subtract).then_inc(W_lo, 1)
                    if q == Y_STEP:
                        y_evac(EB * i + (b + 1), bass.ds(EB * i + b, 1), BODY_PIECES * i + (E_PIECES * b + WR))
                    if q in X_STEP:
                        h = X_STEP.index(q)
                        x_lo((b + 1) % 2, h, 2 * EB * i + (2 * b + h + 3))
                    if q in A_STEP:
                        h = A_STEP.index(q)
                        dve.wait_ge(act_ok, 2 * EB * i + (2 * b + h + 1))
                        dve.tensor_tensor(hrow[:], gate_act[:], bank(2 * h + 1, rows=SL), ALU.mult).then_inc(hrow_ok, 1)
                    if q in T_STEP:
                        h = T_STEP.index(q)
                        dve.wait_ge(ht_hi, 2 * EB * i + (2 * b + h + 1))
                        dve.tensor_tensor(HTl[:, 4 * h:4 * h + 4, :], bank(6, 0, 4 * SL).rearrange("p (k s) -> p k s", k=4),
                                          HTh[:, 4 * h:4 * h + 4, :].bitcast(F32), ALU.subtract).then_inc(ht_lo, 1)
                    p, r = n // 48, n % 48 - CB_START - CB_LAG
                    if r >= 0 and r % CB_EVERY == 0 and r // CB_EVERY < 10:
                        g = r // CB_EVERY
                        dve.wait_ge(cb_ps, 20 * i + (10 * p + g + 1))
                        dst = xt[:, g // 2, 512 * (g % 2):512 * (g % 2) + 512]
                        dve.tensor_tensor(dst, dst, bank(7), ALU.add).then_inc(cb_free, 1)
        y_evac(NE + 1, slice(NE, NE + 1), NE * E_PIECES + WR)
        dve.tensor_scalar(ST[3][:], iota_tok[0:SL, :], idx_slot[:, NE:NE + 1], None, ALU.is_equal)
        dve.wait_ge(y_hi, NE + 1)
        dve.tensor_tensor(Yl[3][:], ysc[:], Yh[3][:].bitcast(F32), ALU.subtract).then_inc(y_lo, 1)

        for c in range(CH + 1):
            if c < CH:
                dve.wait_ge(last_ps, c + 1)
                layer_stats(PS[:, 1024 * (c % 4):1024 * (c % 4) + 1024], c).then_inc(var3_ok, 1)
            if c:
                x = xt[:, c - 1, :]
                dve.wait_ge(norm3_ok, c)
                if c == 1:
                    dve.wait_ge(ln2_in, 32)
                last = dve.tensor_tensor(x, x, ln2g[:], ALU.mult)
                if c - 1 < POOL_LAST:
                    last.then_inc(gain_ok, 1)
                else:
                    link(last)
                    dve.tensor_tensor(x, x, ln2b[:], ALU.add).then_inc(y_out, 1)


_INS = ["x_prompt", "x_sample", "cache_k", "cache_v", "state_h", "c", "c_ctx", "w_mod", "b_mod", "w_in", "q_norm_g",
        "k_norm_g", "conv_w", "conv_b", "w_rg_a", "b_rg_a", "w_rg_x", "b_rg_x", "rg_lambda", "w_out", "ln1_g", "ln1_b",
        "w_router", "w_gate_up", "w_down", "ln2_g", "ln2_b"]
_OUTS = [("y_prompt", (1, N_P, D)), ("y_sample", (1, N_S, D)), ("new_k", (1, 1, N_P, NKV, HD)),
         ("new_v", (1, 1, N_P, NKV, HD)), ("new_h", (1, 1, 2, RG))]


def shape_constants():
    out = np.zeros((P, P + 256 + NT), np.float32)
    out[:, 0:P] = np.eye(P)
    nf = HD // 4
    inv = 10000.0 ** (-np.arange(nf) / nf)
    tok = np.arange(N_S)
    ang = np.concatenate([(tok // GRID_W)[:, None] * inv, (tok % GRID_W)[:, None] * inv], axis=1)
    cs = np.stack([np.cos(ang), np.sin(ang)], axis=1).reshape(4, P, 2, 2 * nf)
    out[:, P:P + 256] = cs.transpose(1, 0, 2, 3).reshape(P, 256)
    out[:, P + 256:] = np.arange(NT)
    return out


def kernel(**inputs):
    import concourse.bacc as bacc
    from concourse.bass_utils import run_bass_kernel_spmd

    nc = bacc.Bacc("TRN2", target_bir_lowering=False, num_devices=1)
    arrays, t = {}, {}
    for name in _INS + ["consts"]:
        a = shape_constants() if name == "consts" else np.ascontiguousarray(inputs[name])
        arrays[f"in_{name}"] = a
        t[name] = nc.dram_tensor(f"in_{name}", a.shape, mybir.dt.from_np(a.dtype), kind="ExternalInput").ap()
    for name, shape in _OUTS:
        t[name] = nc.dram_tensor(f"out_{name}", shape, F32, kind="ExternalOutput").ap()
    build(nc, t)
    r = run_bass_kernel_spmd(nc, [arrays], core_ids=[0])
    return tuple(r.results[0][f"out_{name}"] for name, _ in _OUTS)
```
